# Optimizing a Trainium2 kernel written in Bass

```python
import jax
import jax.numpy as jnp
from jax import lax
import numpy as np

D_MODEL = 1024
BATCH = 1
SEQ = 1024
DEPTH = 1

M_WIDTH = D_MODEL
M_HEADS = 4
M_HEAD_DIM = M_WIDTH // M_HEADS
M_CHUNK = 128
CONV_WIDTH = 4
A_GROUPS = ((128, 1), (512, 4), (2048, 16))
N_GROUPS = 3
A_HEADS_PER_GROUP = 4
A_HEAD_DIM = 128
A_OUT_WIDTH = A_HEADS_PER_GROUP * A_HEAD_DIM
A_QKV_WIDTH = N_GROUPS * A_OUT_WIDTH
A_BLOCK = 128
ROPE_DIM = A_HEAD_DIM // 4
ROPE_THETA = 500000.0
NORM_EPS = 1e-6
NEG_INF = -1e30
IN_SPLITS = (M_WIDTH, M_WIDTH, M_WIDTH, M_WIDTH, M_WIDTH, 2 * M_HEADS, A_QKV_WIDTH, A_QKV_WIDTH, A_QKV_WIDTH, A_OUT_WIDTH, D_MODEL, D_MODEL)
IN_WIDTH = 5 * M_WIDTH + 2 * M_HEADS + 3 * A_QKV_WIDTH + A_OUT_WIDTH + 2 * D_MODEL

kernel_name = 'hybrid_mlstm_dilated_attn_block'

def rmsnorm(x, w):
    xf = x.astype(jnp.float32)
    y = xf * lax.rsqrt(jnp.mean(xf * xf, axis=-1, keepdims=True) + NORM_EPS) * w.astype(jnp.float32)
    return y.astype(x.dtype)

def causal_depthwise_conv(x, w, b):
    C = x.shape[-1]
    y = lax.conv_general_dilated(x, w.astype(x.dtype)[:, None, :], window_strides=(1,), padding=[(CONV_WIDTH - 1, 0)], dimension_numbers=('NWC', 'WIO', 'NWC'), feature_group_count=C)
    return y + b.astype(x.dtype)

def apply_partial_rope(x, cos, sin):
    half = ROPE_DIM // 2
    c = cos[None, :, None, :]
    s = sin[None, :, None, :]
    x1 = x[..., :half]
    x2 = x[..., half:ROPE_DIM]
    return jnp.concatenate([x1 * c - x2 * s, x2 * c + x1 * s, x[..., ROPE_DIM:]], axis=-1)

def mlstm_chunkwise(q, k, v, i_pre, log_f):
    B, H, S, Dk = q.shape
    Dv = v.shape[-1]
    L = M_CHUNK
    nc = S // L
    qc = q.reshape(B, H, nc, L, Dk)
    kc = k.reshape(B, H, nc, L, Dk)
    vc = v.reshape(B, H, nc, L, Dv)
    ic = i_pre.reshape(B, H, nc, L)
    b = jnp.cumsum(log_f.reshape(B, H, nc, L), axis=-1)
    b_tot = b[..., -1]
    a = b_tot[..., None] - b + ic

    def step(carry, inp):
        C, n, m = carry
        k_j, v_j, a_j, bt_j = inp
        m_new = jnp.maximum(bt_j + m, a_j.max(-1))
        decay = jnp.exp(bt_j + m - m_new)
        w = jnp.exp(a_j - m_new[..., None])
        C_new = decay[..., None, None] * C + jnp.einsum('bhl,bhlk,bhlv->bhkv', w, k_j, v_j)
        n_new = decay[..., None] * n + jnp.einsum('bhl,bhlk->bhk', w, k_j)
        return (C_new, n_new, m_new), (C, n, m)

    init = (jnp.zeros((B, H, Dk, Dv), jnp.float32), jnp.zeros((B, H, Dk), jnp.float32), jnp.zeros((B, H), jnp.float32))
    xs = (jnp.moveaxis(kc, 2, 0), jnp.moveaxis(vc, 2, 0), jnp.moveaxis(a, 2, 0), jnp.moveaxis(b_tot, 2, 0))
    _, (C_prev, n_prev, m_prev) = lax.scan(step, init, xs)
    C_prev = jnp.moveaxis(C_prev, 0, 2)
    n_prev = jnp.moveaxis(n_prev, 0, 2)
    m_prev = jnp.moveaxis(m_prev, 0, 2)

    causal = jnp.tril(jnp.ones((L, L), dtype=bool))
    log_d = jnp.where(causal, b[..., :, None] - b[..., None, :] + ic[..., None, :], NEG_INF)
    inter_log = b + m_prev[..., None]
    m_t = jnp.maximum(inter_log, log_d.max(-1))
    s = jnp.einsum('bhnld,bhnsd->bhnls', qc, kc) * jnp.exp(log_d - m_t[..., None])
    inter = jnp.exp(inter_log - m_t)
    num = inter[..., None] * jnp.einsum('bhnld,bhndv->bhnlv', qc, C_prev) + jnp.einsum('bhnls,bhnsv->bhnlv', s, vc)
    den = inter * jnp.einsum('bhnld,bhnd->bhnl', qc, n_prev) + s.sum(-1)
    h = num / jnp.maximum(jnp.abs(den), jnp.exp(-m_t))[..., None]
    return h.reshape(B, H, S, Dv)

def dilated_window_attention(q, k, v, window, dilation):
    B, S, H, Dh = q.shape
    band = window // dilation
    Ls = S // dilation
    nblk = -(-Ls // A_BLOCK)
    Lp = nblk * A_BLOCK

    def by_residue(t):
        return t.reshape(B, Ls, dilation, H, Dh).transpose(0, 2, 3, 1, 4)

    qs, ks, vs = by_residue(q), by_residue(k), by_residue(v)
    qb = jnp.pad(qs, ((0, 0), (0, 0), (0, 0), (0, Lp - Ls), (0, 0))).reshape(B, dilation, H, nblk, A_BLOCK, Dh)

    def key_blocks(t):
        tp = jnp.pad(t, ((0, 0), (0, 0), (0, 0), (A_BLOCK, Lp - Ls), (0, 0)))
        prev = tp[..., :Lp, :].reshape(B, dilation, H, nblk, A_BLOCK, Dh)
        cur = tp[..., A_BLOCK:, :].reshape(B, dilation, H, nblk, A_BLOCK, Dh)
        return jnp.concatenate([prev, cur], axis=-2)

    kb, vb = key_blocks(ks), key_blocks(vs)
    t_idx = jnp.arange(A_BLOCK)[:, None]
    j_idx = jnp.arange(2 * A_BLOCK)[None, :]
    dist = t_idx - j_idx + A_BLOCK
    kpos = jnp.arange(nblk)[:, None, None] * A_BLOCK - A_BLOCK + j_idx[None]
    valid = (dist >= 0) & (dist <= band) & (kpos >= 0)
    s = jnp.einsum('bdhnqe,bdhnke->bdhnqk', qb, kb) * (A_HEAD_DIM ** -0.5)
    s = jnp.where(valid, s, NEG_INF)
    m = s.max(-1)
    p = jnp.where(valid, jnp.exp(s - m[..., None]), 0.0)
    l = p.sum(-1)
    o = jnp.einsum('bdhnqk,bdhnke->bdhnqe', p, vb) / jnp.where(l > 0, l, 1.0)[..., None]
    o = o.reshape(B, dilation, H, Lp, Dh)[..., :Ls, :].transpose(0, 3, 1, 2, 4).reshape(B, S, H, Dh)
    m = m.reshape(B, dilation, H, Lp)[..., :Ls].transpose(0, 3, 1, 2).reshape(B, S, H)
    l = l.reshape(B, dilation, H, Lp)[..., :Ls].transpose(0, 3, 1, 2).reshape(B, S, H)
    return o, m, l

def hybrid_layer(x, pre_w, w_in, b_if, conv_w, conv_b, m_norm_w, w_pm, w_pa, w_out, post_w):
    B, S, _ = x.shape
    f32 = jnp.float32
    h = rmsnorm(x, pre_w)
    proj = h @ w_in.astype(x.dtype)
    idx = np.cumsum(np.array(IN_SPLITS))[:-1].tolist()
    q_m, k_m, v_m, o_m, z_m, if_pre, q_a, k_a, v_a, z_a, g_m, g_a = jnp.split(proj, idx, axis=-1)

    qk = jax.nn.silu(causal_depthwise_conv(jnp.concatenate([q_m, k_m], axis=-1), conv_w, conv_b))
    q_m, k_m = qk[..., :M_WIDTH], qk[..., M_WIDTH:]

    def to_heads(t):
        return t.astype(f32).reshape(B, S, M_HEADS, M_HEAD_DIM).transpose(0, 2, 1, 3)

    gates = if_pre.astype(f32) + b_if.astype(f32)
    i_pre = gates[..., :M_HEADS].transpose(0, 2, 1)
    log_f = jax.nn.log_sigmoid(gates[..., M_HEADS:]).transpose(0, 2, 1)
    hm = mlstm_chunkwise(to_heads(q_m), to_heads(k_m) * (M_HEAD_DIM ** -0.5), to_heads(v_m), i_pre, log_f)
    hm = hm.transpose(0, 2, 1, 3) * jax.nn.sigmoid(o_m.astype(f32)).reshape(B, S, M_HEADS, M_HEAD_DIM)
    hm = hm * lax.rsqrt(jnp.mean(hm * hm, axis=-1, keepdims=True) + NORM_EPS) * m_norm_w.astype(f32).reshape(M_HEADS, M_HEAD_DIM)
    hm = hm.reshape(B, S, M_WIDTH).astype(x.dtype) * jax.nn.silu(z_m)
    branch_m = hm @ w_pm.astype(x.dtype)

    pos = jnp.arange(S, dtype=f32)
    inv_freq = ROPE_THETA ** (-jnp.arange(0, ROPE_DIM, 2, dtype=f32) / ROPE_DIM)
    ang = pos[:, None] * inv_freq[None, :]
    cos, sin = jnp.cos(ang), jnp.sin(ang)
    qa = q_a.astype(f32).reshape(B, S, N_GROUPS, A_HEADS_PER_GROUP, A_HEAD_DIM)
    ka = k_a.astype(f32).reshape(B, S, N_GROUPS, A_HEADS_PER_GROUP, A_HEAD_DIM)
    va = v_a.astype(f32).reshape(B, S, N_GROUPS, A_HEADS_PER_GROUP, A_HEAD_DIM)
    outs, maxes, dens = [], [], []
    for g, (window, dilation) in enumerate(A_GROUPS):
        o, m, l = dilated_window_attention(apply_partial_rope(qa[:, :, g], cos, sin), apply_partial_rope(ka[:, :, g], cos, sin), va[:, :, g], window, dilation)
        outs.append(o)
        maxes.append(m)
        dens.append(l)
    outs = jnp.stack(outs)
    maxes = jnp.stack(maxes)
    dens = jnp.stack(dens)
    wts = jnp.exp(maxes - maxes.max(0, keepdims=True)) * dens
    att = (wts[..., None] * outs).sum(0) / wts.sum(0)[..., None]
    att = att.reshape(B, S, A_OUT_WIDTH).astype(x.dtype) * jax.nn.silu(z_a)
    branch_a = att @ w_pa.astype(x.dtype)

    merged = jax.nn.sigmoid(g_m) * branch_m + jax.nn.sigmoid(g_a) * branch_a
    y = merged @ w_out.astype(x.dtype)
    return x + rmsnorm(y, post_w)

def setup_inputs(seed: int = 0) -> dict:
    key = jax.random.key(seed)
    ks = jax.random.split(key, 12)
    f32 = jnp.float32
    nrm = jax.random.normal
    x = nrm(ks[0], (BATCH, SEQ, D_MODEL), f32)
    pre_norm_w = 1.0 + 0.05 * nrm(ks[1], (DEPTH, D_MODEL), f32)
    w_in = nrm(ks[2], (DEPTH, D_MODEL, IN_WIDTH), f32) * D_MODEL ** -0.5
    b_if = jnp.concatenate([0.1 * nrm(ks[3], (DEPTH, M_HEADS), f32), jnp.linspace(3.0, 6.0, M_HEADS, dtype=f32)[None, :] + 0.1 * nrm(ks[4], (DEPTH, M_HEADS), f32)], axis=-1)
    conv_w = nrm(ks[5], (DEPTH, CONV_WIDTH, 2 * M_WIDTH), f32) * CONV_WIDTH ** -0.5
    conv_b = 0.01 * nrm(ks[6], (DEPTH, 2 * M_WIDTH), f32)
    m_norm_w = 1.0 + 0.05 * nrm(ks[7], (DEPTH, M_WIDTH), f32)
    w_proj_m = nrm(ks[8], (DEPTH, M_WIDTH, D_MODEL), f32) * M_WIDTH ** -0.5
    w_proj_a = nrm(ks[9], (DEPTH, A_OUT_WIDTH, D_MODEL), f32) * A_OUT_WIDTH ** -0.5
    w_out = nrm(ks[10], (DEPTH, D_MODEL, D_MODEL), f32) * D_MODEL ** -0.5
    post_norm_w = 1.0 + 0.05 * nrm(ks[11], (DEPTH, D_MODEL), f32)
    return {'x': x, 'pre_norm_w': pre_norm_w, 'w_in': w_in, 'b_if': b_if, 'conv_w': conv_w, 'conv_b': conv_b, 'm_norm_w': m_norm_w, 'w_proj_m': w_proj_m, 'w_proj_a': w_proj_a, 'w_out': w_out, 'post_norm_w': post_norm_w}

def reference(x, pre_norm_w, w_in, b_if, conv_w, conv_b, m_norm_w, w_proj_m, w_proj_a, w_out, post_norm_w):
    for layer in range(DEPTH):
        x = hybrid_layer(x, pre_norm_w[layer], w_in[layer], b_if[layer], conv_w[layer], conv_b[layer], m_norm_w[layer], w_proj_m[layer], w_proj_a[layer], w_out[layer], post_norm_w[layer])
    return x


_drawn_inputs = setup_inputs


def setup_inputs(seed=0):
    import zlib

    import numpy as np

    out = dict(_drawn_inputs(seed))
    spreads = {}
    factors = {'conv_b': 8.0}
    for name, (base, spread) in spreads.items():
        noise = np.random.default_rng([zlib.crc32(name.encode()), seed]).standard_normal(out[name].shape)
        drawn = base * np.exp(spread * noise) if base else spread * noise
        out[name] = jnp.asarray(drawn.astype(out[name].dtype))
    for name, factor in factors.items():
        out[name] = (out[name] * factor).astype(out[name].dtype)
    return out
```

```python
from contextlib import ExitStack

import numpy as np

import concourse.bass as bass
from concourse import mybir
from concourse.alu_op_type import AluOpType as ALU

ACT = mybir.ActivationFunctionType
AX = mybir.AxisListType
F32 = mybir.dt.float32
F32R = mybir.dt.float32r
BF16 = mybir.dt.bfloat16

P = 128
DM = 1024
S = 1024
KT = DM // P
NT = S // P
MH, MD = 4, 256
AH, AD, NG = 4, 128, 3
AOUT = AH * AD
GROUPS = ((128, 1), (512, 4), (2048, 16))
DIL = [d for _, d in GROUPS]
assert all(w // d == P for w, d in GROUPS)
EPS = 1e-6
NEG = -1.0e30
ASCALE = float(AD) ** -0.5
C_QM, C_KM, C_VM, C_OM, C_ZM = (i * DM for i in range(5))
C_IF = 5 * DM
C_QA = C_IF + 2 * MH
C_KA = C_QA + NG * AOUT
C_VA = C_KA + NG * AOUT
C_ZA = C_VA + NG * AOUT
C_GM = C_ZA + AOUT
C_GA = C_GM + DM

SLOT_QUANTA = (1, 1, 1, 2, 1, 1, 1, 2)
WSLOTS = 4


class Quantum:

    def __init__(self, kind, form, head=0, part=0, tile=0, width=128):
        self.kind, self.form = kind, form
        self.head, self.part, self.tile, self.width = head, part, tile, width


def att_quanta(h):
    out = [Quantum(kind, "T", h, tile=g) for kind in ("va", "ka", "qa") for g in range(NG)]
    return out + [Quantum("za", "T", h)]


def mlstm_quanta(h):
    out = [Quantum("mconv", "T", h, part=p, tile=d) for p in range(2) for d in range(2)]
    out += [Quantum("mo", "N", h, part=i, width=256) for i in range(2)]
    out += [Quantum("mv", "N", h, part=i, width=256) for i in range(2)]
    return out + [Quantum("mz", "T", h, tile=d) for d in range(2)]


def plan():
    quanta, slots = [Quantum("if", "T")], [("start", 0, 0, [0])]

    def take(new):
        first = len(quanta)
        quanta.extend(new)
        return list(range(first, len(quanta)))

    slots += [("fill", 0, i, [q]) for i, q in enumerate(take(att_quanta(0)))]
    gates = [Quantum("gate", "T", tile=t, part=p) for p in range(2) for t in range(KT)]
    for name, count in (("att", AH), ("mlstm", MH)):
        for h in range(count):
            if h + 1 < count:
                new = att_quanta(h + 1) if name == "att" else mlstm_quanta(h + 1)
            else:
                new = mlstm_quanta(0) if name == "att" else gates[:10]
            ids = take(new)
            at = 0
            for n, k in enumerate(SLOT_QUANTA):
                slots.append((name, h, n, ids[at:at + k]))
                at += k
    tail = take(gates[10:] + [Quantum("pa", "T", tile=t) for t in range(KT)]
                + [Quantum("pm", "T", tile=t) for t in range(KT)]
                + [Quantum("y", "N", tile=c, part=i, width=256) for c in range(4) for i in range(2)])
    slots += [("tail", 0, i, [q]) for i, q in enumerate(tail)]
    return quanta, slots



def key_tiles(g, n):
    per_residue = S // DIL[g] // P
    return 2 if per_residue > 1 and n % per_residue else 1


def places(n):
    return (0, key_tiles(0, n), 4)


def hybrid_kernel(nc, x, w_in, w_pm, w_pa, w_out, b_gate, conv_wt, conv_bt, pre_wt, m_wt, post_w,
                  c_ident, c_mask, c_tril, c_rope, out):
    quanta, slots = plan()
    NQ = len(quanta)
    index = {(q.kind, q.head, q.part, q.tile): i for i, q in enumerate(quanta)}
    FIRST_PA = index[("pa", 0, 0, 0)]
    FIRST_PM = index[("pm", 0, 0, 0)]
    FIRST_Y = index[("y", 0, 0, 0)]

    loads = []
    splits_for = {}
    need = {}
    for q in range(NQ):
        mine = []
        if q == FIRST_PA - 1:
            mine += [("att", t) for t in range(AH)]
        if FIRST_PA + 4 <= q < FIRST_PM:
            t = 2 * (q - FIRST_PA - 4)
            mine += [("hm", t), ("hm", t + 1)]
        mine.append(("w", q))
        splits_for[q] = range(len(loads), len(loads) + len(mine))
        loads += mine
    for q in range(NQ):
        last = q + 1 if quanta[q].width == 256 and quanta[q].part == 0 else q
        need[q] = splits_for[last][-1] + 1

    def wslot(q):
        return (q - 1) % WSLOTS

    def chunk_done(q):
        return 1 if q == 0 else 2 * ((q - 1) // 2) + 3

    BY_ACT = {"if", "va", "ka", "qa", "za", "mconv", "mv", "mo", "mz", "gate", "y"}
    BY_DVE = {"za", "mconv", "mz", "pa", "pm"}
    evac_no, post_no = {}, {}
    for i, q in enumerate(quanta):
        evac_no[i] = sum(z.kind in BY_ACT for z in quanta[:i + 1])
        post_no[i] = sum(z.kind in BY_DVE for z in quanta[:i + 1])
    rope_no = {i: sum(z.kind in ("ka", "qa") for z in quanta[:i + 1]) for i in range(NQ)}
    conv_no = {i: sum(z.kind == "mconv" for z in quanta[:i + 1]) for i in range(NQ)}

    bank_no, keep_no = {}, {}

    def number(table, key):
        table[key] = len(table)

    for n2 in range(2):
        for kt in range(KT):
            number(bank_no, ("ht", kt, n2))
    last_qs = []
    for kind, h, n, qs in slots:
        if kind == "att":
            number(bank_no, ("score", h, n, 0))
            number(bank_no, ("score", h, n, 1))
        for q in last_qs:
            if quanta[q].kind == "va":
                number(bank_no, ("vT", q, 0))
                number(bank_no, ("vT", q, 1))
        last_qs = qs
        if kind == "fill" and n == 4:
            for a in range(4):
                for j2 in range(2):
                    number(bank_no, ("cols", a, j2))
            number(bank_no, ("decay",))
        if kind == "att":
            number(bank_no, ("probT", h, n, 0))
            number(bank_no, ("probT", h, n, 1))
        if (kind == "mlstm" and h and n == 1) or (kind == "tail" and n == 1):
            hp = h - 1 if kind == "mlstm" else MH - 1
            for d in range(2):
                for j2 in range(2):
                    number(bank_no, ("hmT", hp, d, j2))
        if kind == "mlstm":
            number(bank_no, ("qk", h, n))
            if n < NT - 1:
                number(keep_no, ("k", h, n))
            if n:
                number(keep_no, ("A", h, n))
            number(bank_no, ("B", h, n))
            if n < NT - 1:
                number(bank_no, ("C", h, n, 0))
                number(bank_no, ("C", h, n, 1))

    ctx = ExitStack()
    with ctx:
        at0 = (nc.sbuf_base + 63) // 64 * 64
        A_H = at0
        A_W = A_H + 2 * KT * S * 4
        A_D = A_W + (2 + 2 * WSLOTS) * 4096
        VE = MD + 1
        SET = (4 * 8192 + NT * VE * 4 + 63) // 64 * 64
        A_E = A_D + 2 * SET

        def at(name, shape, dt, offset):
            return nc.alloc_sbuf_tensor_at(name, shape, dt, offset=offset)

        hhi = at("hhi", [P, KT, S], F32R, A_H)
        hlo = at("hlo", [P, KT, S], F32R, A_H + KT * S * 4)
        raw = at("raw", [P, 2, KT, P], F32, A_W)
        whi = at("whi", [P, WSLOTS, KT, P], F32R, A_W + 2 * 4096)
        wlo = at("wlo", [P, WSLOTS, KT, P], F32R, A_W + (2 + WSLOTS) * 4096)

        ka_sb, va_sb, qa_sb, za_sb, mqk, mv_sb, mo_sb, mz_sb = [], [], [], [], [], [], [], []
        for i in range(2):
            b = A_D + i * SET
            ka_sb.append(at(f"ka{i}", [P, NG, S], F32, b))
            va_sb.append(at(f"va{i}", [P, NG, S], F32, b + NG * 4096))
            qa_sb.append(at(f"qa{i}", [P, NG, S], F32, b + 2 * NG * 4096))
            za_sb.append(at(f"za{i}", [P, S], F32, b + 3 * NG * 4096))
            mqk.append(at(f"mqk{i}", [P, 2, 2, S], F32, b))
            mo_sb.append(at(f"mo{i}", [P, NT, MD], F32, b + 16384))
            mv_sb.append(at(f"mv{i}", [P, NT, VE], F32, b + 24576))
            mz_sb.append(at(f"mz{i}", [P, 2, S], F32, b + SET - 8192))
        x_sb = at("x_sb", [P, NT, DM], F32, A_D)
        rows = [at(f"row{i}", [P, S], F32, A_D + SET + i * 4096) for i in range(10)]
        gm_sb = at("gm_sb", [P, KT, S], F32, A_D)
        ga_sb = at("ga_sb", [P, KT, S], F32, A_D + KT * 4096)
        mghi = at("mghi", [P, KT, S], F32R, A_D)
        mglo = at("mglo", [P, KT, S], F32R, A_D + KT * 4096)
        athi = at("athi", [P, AH, S], F32R, A_D + 2 * KT * 4096)
        atlo = at("atlo", [P, AH, S], F32R, A_D + 2 * KT * 4096 + AH * 4096)
        hmhi = at("hmhi", [P, KT, S], F32R, A_H)
        hmlo = at("hmlo", [P, KT, S], F32R, A_H + KT * S * 4)
        y_sb = at("y_sb", [P, NT, DM], F32, A_H)
        x2_sb = at("x2_sb", [P, NT, DM], F32, A_H + NT * DM * 4)
        pw_sb = at("pw_sb", [P, DM], F32, A_D + 2 * KT * 4096)

        pos = [A_E]

        def small(name, shape, dt, size=4):
            t = at(name, shape, dt, pos[0])
            pos[0] += (int(np.prod(shape[1:])) * size + 31) // 32 * 32
            return t

        rope_sb = small("rope_sb", [64, S], F32)
        share_sb = small("share_sb", [P, NG, S], F32)
        assert A_D + 2 * KT * 4096 + 2 * AH * 4096 <= pos[0]
        mask_sb = small("mask_sb", [P, 3 * P], BF16, 2)
        A_M = pos[0]
        prob = small("prob", [P, 2, 5 * P], F32)
        probT = small("probT", [P, 2, 5 * P], F32)
        ml = small("ml", [P, 2, NG, NT, 2], F32)
        mlc = at("mlc", [NT, NG, P, 2], F32, A_E + 4096)
        lead = at("lead", [NT, 2, P], F32, A_E + 4096 + 3072)
        eg = at("eg", [NT, 3, NG, P], F32, A_E + 4096 + 4096)
        tmp = small("tmp", [P, S], F32)
        ident = small("ident", [P, P], F32)
        tril = small("tril", [P, P], F32)
        negg = small("negg", [P, S], F32)
        cols = small("cols", [P, 4, NT, MH], F32)
        decay = small("decay", [P, MH, NT], F32)
        cw = small("cw", [P, 16, 4], F32)
        cb = small("cb", [P, 16], F32)
        prew = small("prew", [P, KT], F32)
        mw = small("mw", [P, KT], F32)
        bg = small("bg", [P, 2], F32)
        ifw = small("ifw", [P, KT, 2 * MH], F32)
        srow = small("srow", [P, 8, NT], F32)
        halfneg = small("halfneg", [P, NT], F32)
        ssq = small("ssq", [P, 2 * NT], F32)
        pmax = small("pmax", [P, 8], F32)
        den = small("den", [P, 2], F32)
        rden = small("rden", [P, NT], F32)
        msq = small("msq", [P, NT], F32)
        mrs = small("mrs", [P, NT], F32)
        ysq = small("ysq", [P, NT, 4], F32)
        ysum = small("ysum", [P, NT], F32)
        yrs = small("yrs", [P, NT], F32)
        junk = tmp
        mfac = small("mfac", [P, NT], F32)
        end, pos[0] = pos[0], A_M
        state = small("state", [P, 2, VE], F32)
        kw = small("kw", [P, MD], F32)
        dmat = small("dmat", [P, P], F32)
        emat = small("emat", [P, P], F32)
        wmat = small("wmat", [P, P], F32)
        inter = small("inter", [P, VE], F32)
        total = small("total", [P, VE], F32)
        sq_junk = small("sq_junk", [P, MD], F32)
        assert pos[0] <= A_M + 2 * 2 * 5 * P * 4
        pos[0] = end
        assert pos[0] <= nc.sbuf_usable_end, (pos[0], nc.sbuf_usable_end)

        proj = ctx.enter_context(nc.psum_tensor("proj", [P, 2, 1024], F32))
        bank = [ctx.enter_context(nc.psum_tensor(f"bank{i}", [P, 512], F32)) for i in range(3)]
        keep = ctx.enter_context(nc.psum_tensor("keep", [P, 512], F32))

        att_dram = nc.dram_tensor("att_spill", [AOUT, S], F32).ap()
        hm_dram = nc.dram_tensor("hm_spill", [DM, S], F32).ap()
        ml_dram = nc.dram_tensor("ml_spill", [AH, NG, S, 2], F32).ap()
        share_dram = nc.dram_tensor("share_spill", [AH, NG, S], F32).ap()

        def sem(name):
            return ctx.enter_context(nc.semaphore(name))

        x_in = [sem(f"x_in{i}") for i in range(NT)]
        start_in = sem("start_in")
        const_in = sem("const_in")
        NSTART, NCONST = 3, 7
        raw_in = [sem(f"raw_in{i}") for i in range(2)]
        att_out = sem("att_out")
        hm_out = sem("hm_out")
        ml_out = sem("ml_out")
        ml_in = sem("ml_in")
        share_out = sem("share_out")
        share_in = sem("share_in")
        x2_in = sem("x2_in")
        y_out = sem("y_out")
        pe_quantum = sem("pe_quantum")
        pe_bank = sem("pe_bank")
        pe_keep = sem("pe_keep")
        pe_pv = sem("pe_pv")
        hi_done = sem("hi_done")
        ht_hi = sem("ht_hi")
        evac = sem("evac")
        a_step = sem("a_step")
        x_sq = sem("x_sq")
        log_done = sem("log_done")
        dec_exp = sem("dec_exp")
        cols_exp = sem("cols_exp")
        p_exp = sem("p_exp")
        out_done = sem("out_done")
        eg_done = sem("eg_done")
        tanh_done = sem("tanh_done")
        kw_done = sem("kw_done")
        inter_done = sem("inter_done")
        e_done = sem("e_done")
        sq_done = sem("sq_done")
        mg_hi = sem("mg_hi")
        v_step = sem("v_step")
        if_ready = sem("if_ready")
        x_ms = sem("x_ms")
        x_norm = sem("x_norm")
        bank_free = sem("bank_free")
        f_ready = sem("f_ready")
        rows_ready = sem("rows_ready")
        post = sem("post")
        rope_done = sem("rope_done")
        silu_done = sem("silu_done")
        max_done = sem("max_done")
        lead_done = sem("lead_done")
        share_done = sem("share_done")
        att_done = sem("att_done")
        d_done = sem("d_done")
        cw_ready = sem("cw_ready")
        ones_done = sem("ones_done")
        chunk_ready = sem("chunk_ready")
        m_ms = sem("m_ms")
        m_norm = sem("m_norm")
        sum_done = sem("sum_done")
        mg_lo = sem("mg_lo")
        y_ms = sem("y_ms")
        y_done = sem("y_done")
        lo_done = sem("lo_done")
        g_ready = sem("g_ready")
        x_rs = sem("x_rs")
        m_rs = sem("m_rs")
        y_rs = sem("y_rs")

        block = ctx.enter_context(nc.Block())

        def tcol(t):
            return proj[:, t % 2, :]

        @block.sync
        def _(sp):
            for t in range(NT):
                if t == 1:
                    sp.dma_start(ident[:], c_ident).then_inc(start_in, 16)
                    sp.dma_start(prew[:], pre_wt).then_inc(start_in, 16)
                    sp.dma_start(ifw[:], w_in[:, C_IF:C_IF + 2 * MH].rearrange("(k p) c -> p k c", p=P)
                                 ).then_inc(start_in, 16)
                sp.dma_start(x_sb[:, t, :], x[t * P:(t + 1) * P, :]).then_inc(x_in[t], 16)
            for dst, src in ((bg, b_gate), (cw, conv_wt), (cb, conv_bt), (mw, m_wt), (tril, c_tril),
                             (mask_sb, c_mask), (rope_sb, c_rope)):
                into = dst[:].bitcast(mybir.dt.uint16) if dst is mask_sb else dst[:]
                sp.dma_start(into, src).then_inc(const_in, 16)

            def columns(q):
                z = quanta[q]
                h, p, t = z.head, z.part, z.tile
                if z.kind in ("qa", "ka", "va"):
                    return w_in, {"qa": C_QA, "ka": C_KA, "va": C_VA}[z.kind] + t * AOUT + h * AD
                if z.kind == "za":
                    return w_in, C_ZA + h * AD
                if z.kind == "mconv":
                    return w_in, (C_QM, C_KM)[p] + h * MD + t * P
                if z.kind in ("mv", "mo"):
                    return w_in, (C_VM if z.kind == "mv" else C_OM) + h * MD + p * P
                if z.kind == "mz":
                    return w_in, C_ZM + h * MD + t * P
                if z.kind == "gate":
                    return w_in, (C_GM, C_GA)[p] + t * P
                if z.kind == "pa":
                    return w_pa, t * P
                if z.kind == "pm":
                    return w_pm, t * P
                return w_out, z.tile * 256 + z.part * P

            def att_exchange(h, at):
                if at == 3:
                    sp.wait_ge(p_exp, NG * NT * (h + 1))
                    sp.dma_start(ml_dram[h].rearrange("g (n p) c -> p (g n) c", p=P),
                                 ml[:, h % 2].rearrange("p g n c -> p (g n) c")).then_inc(ml_out, 16)
                if at == 4:
                    sp.wait_ge(ml_out, 16 * (h + 1))
                    if h:
                        sp.wait_ge(att_done, h)
                    for g, d in enumerate(DIL):
                        sp.dma_start(mlc[:, g].rearrange("t (l r) c -> t l r c", r=d),
                                     ml_dram[h, g].rearrange("(r t l) c -> t l r c", r=d, t=NT)
                                     ).then_inc(ml_in, 16)
                if at == 7:
                    sp.wait_ge(share_done, h + 1)
                    sp.dma_start(share_dram[h].rearrange("g (t l) -> t g l", t=NT), eg[:, 2]
                                 ).then_inc(share_out, 16)
                if at == 8:
                    sp.wait_ge(share_out, 16 * (h + 1))
                    sp.dma_start(share_sb[:].rearrange("p g s -> p (g s)"),
                                 share_dram[h].rearrange("g s -> (g s)").partition_broadcast(P)
                                 ).then_inc(share_in, 16)

            for r, (what, i) in enumerate(loads):
                if r == 0:
                    continue
                if what == "w":
                    for h in range(AH):
                        first = index[("va", h + 2, 0, 0)] if h < AH - 2 else index[("mconv", h - AH + 2, 0, 0)]
                        att_exchange(h, i - first)
                        if i == first + 10:
                            sp.wait_ge(att_done, h + 1)
                            sp.dma_start(att_dram[h * P:(h + 1) * P, :], za_sb[h % 2][:]
                                         ).then_inc(att_out, 16)
                    for h in range(MH):
                        mark = index[("mo", h + 2, 0, 0)] if h < MH - 2 else (
                            index[("gate", 0, 0, 4)] if h == MH - 2 else FIRST_PA - 2)
                        if i == mark:
                            sp.wait_ge(bank_free, bank_no[("hmT", h, 1, 1)] + 1)
                            sp.dma_start(hm_dram[h * MD:(h + 1) * MD, :].rearrange("(d p) s -> p d s", p=P),
                                         mz_sb[h % 2][:]).then_inc(hm_out, 16)
                slot = r % 2
                if r >= 2:
                    sp.wait_ge(hi_done, r - 1)
                    sp.wait_ge(lo_done, r - 1)
                if what == "w":
                    src, c = columns(i)
                    k = src.shape[0] // P
                    sp.dma_start(raw[:, slot, 0:k, :], src[:, c:c + P].rearrange("(k p) c -> p k c", p=P)
                                 ).then_inc(raw_in[slot], 16)
                else:
                    if what == "att":
                        sp.wait_ge(att_out, 16 * AH)
                        src = att_dram
                    else:
                        sp.wait_ge(hm_out, 16 * MH)
                        src = hm_dram
                    sp.dma_start(raw[:, slot, :, :].rearrange("p k c -> p (k c)"), src[i * P:(i + 1) * P, :]
                                 ).then_inc(raw_in[slot], 16)
            sp.wait_ge(pe_quantum, FIRST_Y)
            sp.dma_start(x2_sb[:], x.rearrange("(t p) d -> p t d", p=P)).then_inc(x2_in, 16)
            sp.dma_start(pw_sb[:], post_w.partition_broadcast(P)).then_inc(x2_in, 16)
            for t in range(NT):
                sp.wait_ge(y_done, t + 1)
                sp.dma_start(out[t * P:(t + 1) * P, :], y_sb[:, t, :]).then_inc(y_out, 16)
            sp.wait_ge(y_out, 16 * NT)

        def raw_wait(eng, r):
            if r == 0:
                eng.wait_ge(if_ready, 1)
            else:
                slot = r % 2
                eng.wait_ge(raw_in[slot], 16 * (r // 2 + (1 if slot else 0)))

        def split_views(r):
            what, i = loads[r]
            src = raw[:, r % 2, :, :]
            if what == "w":
                k = AH if quanta[i].kind == "pa" else KT
                return src[:, 0:k, :], whi[:, wslot(i), 0:k, :], wlo[:, wslot(i), 0:k, :]
            flat = src.rearrange("p k c -> p (k c)")
            return (flat, athi[:, i, :], atlo[:, i, :]) if what == "att" else (flat, hmhi[:, i, :], hmlo[:, i, :])

        def split_target_wait(eng, r):
            what, i = loads[r]
            if what == "w":
                if i >= WSLOTS:
                    eng.wait_ge(pe_quantum, chunk_done(i - WSLOTS))
            elif what == "att":
                eng.wait_ge(hm_out, 16 * MH)
            else:
                eng.wait_ge(pe_quantum, FIRST_PA)

        @block.gpsimd
        def _(g):
            nc.gpsimd.memset(raw[:, 0, :, :], 0.0).then_inc(g_ready, 1)
            nc.gpsimd.memset(halfneg[:], -0.5).then_inc(g_ready, 1)

            def lo(r):
                src, hi, low = split_views(r)
                raw_wait(g, r)
                g.wait_ge(hi_done, r + 1)
                nc.gpsimd.tensor_tensor(low, src, hi.bitcast(F32), ALU.subtract).then_inc(lo_done, 1)

            g.wait_ge(g_ready, 2)
            for i in range(2):
                g.wait_ge(x_ms, i + 1)
                nc.gpsimd.tensor_tensor(ssq[:, NT + 4 * i:NT + 4 * i + 4], ssq[:, 4 * i:4 * i + 4],
                                        halfneg[:, 0:4], ALU.pow).then_inc(x_rs, 1)
            for q in range(3):
                for r in splits_for[q]:
                    lo(r)
            for kind, h, n, qs in slots:
                if (kind == "mlstm" and h and n == 0) or (kind == "tail" and n == 0):
                    hp = h - 1 if kind == "mlstm" else MH - 1
                    g.wait_ge(m_ms, hp + 1)
                    nc.gpsimd.tensor_tensor(mrs[:], msq[:], halfneg[:], ALU.pow).then_inc(m_rs, 1)
                for q in qs:
                    for r in splits_for.get(q + 3, ()):
                        lo(r)
            for i in range(2):
                g.wait_ge(y_ms, i + 1)
                nc.gpsimd.tensor_tensor(yrs[:, 4 * i:4 * i + 4], ysum[:, 4 * i:4 * i + 4],
                                        halfneg[:, 0:4], ALU.pow).then_inc(y_rs, 1)

        @block.tensor
        def _(pe):
            fills = [0]

            def work(key):
                i = bank_no[key]
                assert i == fills[0]
                fills[0] += 1
                if i >= 3:
                    pe.wait_ge(bank_free, i - 2)
                return bank[i % 3]

            def quantum(q):
                z = quanta[q]
                pe.wait_ge(lo_done, need[q])
                if q >= 2:
                    if quanta[q - 2].kind in BY_DVE:
                        pe.wait_ge(post, post_no[q - 2])
                    else:
                        pe.wait_ge(evac, evac_no[q - 2])
                ws = wslot(q)
                slot = tcol(q)
                if z.form == "T":
                    mhi, mlo, k = hhi, hlo, KT
                    if z.kind == "pa":
                        mhi, mlo, k = athi, atlo, AH
                    if z.kind == "pm":
                        mhi, mlo = hmhi, hmlo
                    for kt in range(k):
                        for w, m in ((whi, mhi), (whi, mlo), (wlo, mhi)):
                            for half in range(2):
                                mm = pe.matmul(slot[:, half * 512:(half + 1) * 512], w[:, ws, kt, :],
                                               m[:, kt, half * 512:(half + 1) * 512],
                                               start=(kt == 0 and w is whi and m is mhi),
                                               stop=(kt == k - 1 and w is wlo))
                else:
                    shi, slo = (mghi, mglo) if z.kind == "y" else (hhi, hlo)
                    if z.kind == "y":
                        pe.wait_ge(mg_lo, KT)
                    count = 1024 // z.width
                    first = z.part * count if z.width == 256 else 0
                    if z.width == 256:
                        ws = wslot(q - z.part)
                    for i in range(count):
                        t = first + i
                        for kt in range(KT):
                            for s, w in ((shi, whi), (shi, wlo), (slo, whi)):
                                rhs = w[:, ws:ws + 2, kt, :] if z.width == 256 else w[:, ws, kt, :]
                                mm = pe.matmul(slot[:, i * z.width:(i + 1) * z.width],
                                               s[:, kt, t * P:(t + 1) * P], rhs,
                                               start=(kt == 0 and s is shi and w is whi),
                                               stop=(kt == KT - 1 and s is slo))
                mm.then_inc(pe_quantum, 1)

            def scores(h, n):
                pe.wait_ge(rope_done, rope_no[index[("qa", h, 0, NG - 1)]])
                for g in range(NG):
                    if g != 1:
                        b = work(("score", h, n, g // 2))
                    m, place = key_tiles(g, n), places(n)[g] % 4
                    mm = pe.matmul(b[:, place * P:(place + m) * P], qa_sb[h % 2][:, g, n * P:(n + 1) * P],
                                   ka_sb[h % 2][:, g, (n + 1 - m) * P:(n + 1) * P], start=True, stop=True)
                    if g:
                        mm.then_inc(pe_bank, 1)

            def probabilities(h, n):
                pe.wait_ge(p_exp, NG * (NT * h + n + 1))
                count = places(n)[1] + key_tiles(1, n)
                b = work(("probT", h, n, 0))
                for i in range(count):
                    mm = pe.transpose(b[:, i * P:(i + 1) * P], prob[:, n % 2, i * P:(i + 1) * P], ident[:])
                mm.then_inc(pe_bank, 1)
                b = work(("probT", h, n, 1))
                pe.transpose(b[:, 0:P], prob[:, n % 2, 4 * P:5 * P], ident[:]).then_inc(pe_bank, 1)

            def weigh(h, n):
                pe.wait_ge(bank_free, bank_no[("probT", h, n, 1)] + 1)
                if NT * h + n:
                    pe.wait_ge(out_done, NT * h + n)
                for g in range(NG):
                    m, place = key_tiles(g, n), places(n)[g]
                    for i in range(m):
                        k = n + 1 - m + i
                        mm = pe.matmul(keep[:, g * P:(g + 1) * P], va_sb[h % 2][:, g, k * P:(k + 1) * P],
                                       probT[:, n % 2, (place + i) * P:(place + i + 1) * P],
                                       start=(i == 0), stop=(i == m - 1))
                mm.then_inc(pe_pv, 1)

            def turn_values(q):
                z = quanta[q]
                pe.wait_ge(evac, evac_no[q])
                for j2 in range(2):
                    b = work(("vT", q, j2))
                    for i in range(4):
                        t = 4 * j2 + i
                        mm = pe.transpose(b[:, i * P:(i + 1) * P],
                                          ka_sb[z.head % 2][:, z.tile, t * P:(t + 1) * P], ident[:])
                    mm.then_inc(pe_bank, 1)

            def spread(h):
                return ident[:, 32 * h:32 * h + 1].broadcast_to([P, P])

            def keep_wait(i):
                for kind, done in (("k", kw_done), ("A", inter_done)):
                    before = sum(k[0] == kind for k, v in keep_no.items() if v < i)
                    if before:
                        pe.wait_ge(done, before)

            def chunk_start(h, j):
                qk = mqk[h % 2]
                pe.wait_ge(silu_done, conv_no[index[("mconv", h, 1, 1)]])
                if h == 0 and j == 0:
                    pe.wait_ge(out_done, AH * NT)
                tok = slice(j * P, (j + 1) * P)
                b = work(("qk", h, j))
                for d in range(2):
                    pe.matmul(b[:, 0:P], qk[:, 1, d, tok], qk[:, 0, d, tok], start=(d == 0), stop=(d == 1))
                pe.matmul(b[:, P:2 * P], spread(h), negg[:, tok], start=True, stop=True).then_inc(pe_bank, 1)
                if j < NT - 1:
                    keep_wait(keep_no[("k", h, j)])
                    for d in range(2):
                        mm = pe.transpose(keep[:, d * P:(d + 1) * P], qk[:, 1, d, tok], ident[:])
                    mm.then_inc(pe_keep, 1)

            def state_part(h, j):
                qk = mqk[h % 2]
                tok = slice(j * P, (j + 1) * P)
                if j:
                    keep_wait(keep_no[("A", h, j)])
                    pe.wait_ge(bank_free, bank_no[("C", h, j - 1, 1)] + 1)
                    for d in range(2):
                        mm = pe.matmul(keep[:, 0:VE], qk[:, 0, d, tok], state[:, d, :],
                                       start=(d == 0), stop=(d == 1))
                    mm.then_inc(pe_keep, 1)

            def chunk_end(h, j):
                v = mv_sb[h % 2]
                pe.wait_ge(bank_free, bank_no[("qk", h, j)] + 1)
                if j == 0:
                    pe.wait_ge(evac, evac_no[index[("mv", h, 1, 0)]])
                    pe.wait_ge(ones_done, h + 1)
                b = work(("B", h, j))
                pe.matmul(b[:, 0:VE], wmat[:], v[:, j, :], start=True, stop=True).then_inc(pe_bank, 1)
                if j < NT - 1:
                    pe.wait_ge(kw_done, (NT - 1) * h + j + 1)
                    for d in range(2):
                        b = work(("C", h, j, d))
                        pe.matmul(b[:, 0:VE], kw[:, d * P:(d + 1) * P], v[:, j, :],
                                  start=True, stop=True).then_inc(pe_bank, 1)

            def head_output(h):
                pe.wait_ge(m_norm, h + 1)
                for d in range(2):
                    for j2 in range(2):
                        b = work(("hmT", h, d, j2))
                        for i in range(4):
                            mm = pe.transpose(b[:, i * P:(i + 1) * P],
                                              mo_sb[h % 2][:, 4 * j2 + i, d * P:(d + 1) * P], ident[:])
                        mm.then_inc(pe_bank, 1)

            pe.wait_ge(start_in, 16 * NSTART)
            for n2 in range(2):
                for i in range(4):
                    pe.wait_ge(x_norm, 4 * n2 + i + 1)
                for kt in range(KT):
                    b = work(("ht", kt, n2))
                    for i in range(4):
                        mm = pe.transpose(b[:, i * P:(i + 1) * P],
                                          x_sb[:, 4 * n2 + i, kt * P:(kt + 1) * P], ident[:])
                    mm.then_inc(pe_bank, 1)
            pe.wait_ge(bank_free, 2 * KT)
            last_qs = []
            for kind, h, n, qs in slots:
                if kind == "att":
                    scores(h, n)
                    if n:
                        weigh(h, n - 1)
                    elif h:
                        weigh(h - 1, NT - 1)
                if kind == "mlstm" and h == 0 and n == 0:
                    weigh(AH - 1, NT - 1)
                for q in last_qs:
                    if quanta[q].kind == "va":
                        turn_values(q)
                last_qs = qs
                if (kind == "mlstm" and h and n == 1) or (kind == "tail" and n == 1):
                    head_output(h - 1 if kind == "mlstm" else MH - 1)
                if kind == "mlstm":
                    chunk_start(h, n)
                if kind == "fill" and n == 4:
                    pe.wait_ge(rows_ready, 1)
                    for a, r in enumerate((rows[6], rows[0], rows[3], rows[2])):
                        for j2 in range(2):
                            b = work(("cols", a, j2))
                            for i in range(4):
                                j = 4 * j2 + i
                                mm = pe.transpose(b[:, i * P:(i + 1) * P], r[:, j * P:(j + 1) * P], ident[:])
                            mm.then_inc(pe_bank, 1)
                    pe.wait_ge(dec_exp, 1)
                    b = work(("decay",))
                    for hh in range(MH):
                        mm = pe.matmul(b[:, hh * NT:(hh + 1) * NT], spread(hh), srow[:, 5, :],
                                       start=True, stop=True)
                    mm.then_inc(pe_bank, 1)
                for q in qs:
                    quantum(q)
                if kind == "att":
                    probabilities(h, n)
                if kind == "mlstm":
                    state_part(h, n)
                    chunk_end(h, n)

        @block.scalar
        def _(act):
            steps = [0]

            def step(ins):
                ins.then_inc(a_step, 1)
                steps[0] += 1
                act.wait_ge(a_step, steps[0])

            def hi(r):
                src, h, _ = split_views(r)
                raw_wait(act, r)
                split_target_wait(act, r)
                nc.scalar.activation(h, src, ACT.Copy).then_inc(hi_done, 1)

            def take(q):
                z = quanta[q]
                if z.kind not in BY_ACT:
                    return
                act.wait_ge(pe_quantum, q + 1)
                slot = tcol(q)
                s = z.head % 2
                if z.kind == "if":
                    ins = nc.scalar.activation(rows[0][:], slot, ACT.Copy)
                elif z.kind in ("va", "ka", "qa"):
                    if z.kind == "qa" and z.head >= 2:
                        act.wait_ge(att_done, z.head - 1)
                    dst = (qa_sb if z.kind == "qa" else ka_sb)[s][:, z.tile, :]
                    ins = nc.scalar.activation(dst.rearrange("p (r u) -> p r u", r=DIL[z.tile]),
                                               slot.rearrange("p (u r) -> p r u", r=DIL[z.tile]), ACT.Copy)
                elif z.kind == "za":
                    if z.head >= 2:
                        act.wait_ge(att_out, 16 * (z.head - 1))
                    ins = nc.scalar.activation(za_sb[s][:], slot, ACT.Tanh, scale=0.5)
                elif z.kind == "mconv":
                    t = z.part * KT + z.head * 2 + z.tile
                    act.wait_ge(cw_ready, 1)
                    ins = nc.scalar.activation(mqk[s][:, z.part, z.tile, :], slot, ACT.Identity,
                                               bias=cb[:, t:t + 1], scale=cw[:, t, 3:4])
                elif z.kind == "mv":
                    if z.head < 2:
                        act.wait_ge(att_done, z.head + 3)
                    ins = nc.scalar.activation(mv_sb[s][:, 4 * z.part:4 * z.part + 4, 0:MD],
                                               slot.rearrange("p (n c) -> p n c", c=MD), ACT.Copy)
                elif z.kind == "mo":
                    ins = nc.scalar.activation(mo_sb[s][:, 4 * z.part:4 * z.part + 4, :],
                                               slot.rearrange("p (n c) -> p n c", c=MD), ACT.Tanh, scale=0.5)
                elif z.kind == "mz":
                    if z.head >= 2:
                        act.wait_ge(hm_out, 16 * (z.head - 1))
                    else:
                        act.wait_ge(att_out, 16 * (z.head + 3))
                    ins = nc.scalar.activation(mz_sb[s][:, z.tile, :], slot, ACT.Tanh, scale=0.5)
                elif z.kind == "gate":
                    dst = (gm_sb, ga_sb)[z.part]
                    if z.part == 1 and z.tile == 0:
                        act.wait_ge(hm_out, 16 * (MH - 1))
                    ins = nc.scalar.activation(dst[:, z.tile, :], slot, ACT.Tanh, scale=0.5)
                else:
                    ins = nc.scalar.activation(y_sb[:, 4 * z.part:4 * z.part + 4, z.tile * 256:(z.tile + 1) * 256],
                                               slot.rearrange("p (n c) -> p n c", c=256), ACT.Copy)
                ins.then_inc(evac, 1)
                if z.kind == "y":
                    act.wait_ge(evac, evac_no[q])
                    act.wait_ge(sq_done, MH * NT + 4 * (q - FIRST_Y))
                    for i in range(4):
                        t = 4 * z.part + i
                        nc.scalar.activation(junk[:, 256 * i:256 * i + 256],
                                             y_sb[:, t, z.tile * 256:(z.tile + 1) * 256], ACT.Square,
                                             accum_out=ysq[:, t, z.tile:z.tile + 1]).then_inc(sq_done, 1)

            def output(h, n):
                act.wait_ge(pe_pv, NT * h + n + 1)
                nc.scalar.activation(qa_sb[h % 2][:, :, n * P:(n + 1) * P],
                                     keep[:, 0:NG * P].rearrange("p (g q) -> p g q", q=P), ACT.Copy
                                     ).then_inc(out_done, 1)

            def late(q):
                z = quanta[q]
                if z.kind == "mconv":
                    n = conv_no[q]
                    act.wait_ge(post, post_no[q])
                    if n > 1:
                        act.wait_ge(silu_done, n - 1)
                    nc.scalar.activation(tmp[:], mqk[z.head % 2][:, z.part, z.tile, :], ACT.Tanh,
                                         scale=(1.0, 16.0)[z.part]).then_inc(tanh_done, 1)
                if z.kind == "pm":
                    act.wait_ge(sum_done, z.tile + 1)
                    nc.scalar.activation(mghi[:, z.tile, :], ga_sb[:, z.tile, :], ACT.Copy,
                                         scale=0.5).then_inc(mg_hi, 1)

            for t in range(NT):
                act.wait_ge(x_in[t], 16)
                if t:
                    act.wait_ge(x_sq, t)
                nc.scalar.activation(junk[:], x_sb[:, t, :], ACT.Square, accum_out=ssq[:, t:t + 1]
                                     ).then_inc(x_sq, 1)
            act.wait_ge(start_in, 16 * NSTART)
            for n2 in range(2):
                for kt in range(KT):
                    i = bank_no[("ht", kt, n2)]
                    act.wait_ge(pe_bank, i + 1)
                    nc.scalar.activation(hhi[:, kt, n2 * 512:(n2 + 1) * 512], bank[i % 3][:], ACT.Copy,
                                         scale=prew[:, kt:kt + 1]).then_inc(ht_hi, 1)
                    if n2 == 1 and kt in (0, 3, 6):
                        for r in splits_for[kt // 3]:
                            hi(r)
            waiting = []
            for kind, h, n, qs in slots:
                if kind == "att":
                    act.wait_ge(max_done, NT * h + n + 1)
                    for g in range(NG):
                        p = prob[:, n % 2, places(n)[g] * P:(places(n)[g] + key_tiles(g, n)) * P]
                        nc.scalar.activation(p, p, ACT.Exp, bias=ml[:, h % 2, g, n, 0:1], scale=ASCALE,
                                             accum_out=ml[:, h % 2, g, n, 1:2]).then_inc(p_exp, 1)
                    if n:
                        output(h, n - 1)
                    elif h:
                        output(h - 1, NT - 1)
                if kind == "mlstm" and h == 0 and n == 0:
                    output(AH - 1, NT - 1)
                if n == 1 and ((kind == "att" and h) or (kind == "mlstm" and h == 0)):
                    act.wait_ge(lead_done, h if kind == "att" else AH)
                    nc.scalar.activation(eg[:, 0], eg[:, 0], ACT.Exp).then_inc(eg_done, 1)
                if kind == "mlstm":
                    c = NT * h + n
                    if n < NT - 1:
                        act.wait_ge(pe_keep, keep_no[("k", h, n)] + 1)
                        if n:
                            act.wait_ge(pe_bank, bank_no[("C", h, n - 1, 1)] + 1)
                        elif h:
                            act.wait_ge(pe_bank, bank_no[("C", h - 1, NT - 2, 1)] + 1)
                        else:
                            act.wait_ge(cols_exp, 1)
                        nc.scalar.activation(kw[:], keep[:, 0:MD], ACT.Copy, scale=cols[:, 2, n, h:h + 1]
                                             ).then_inc(kw_done, 1)
                    act.wait_ge(d_done, c + 1)
                    nc.scalar.activation(emat[:], dmat[:], ACT.Exp, bias=cols[:, 0, n, h:h + 1]
                                         ).then_inc(e_done, 1)
                    if n:
                        act.wait_ge(chunk_ready, c)
                        if c > 1:
                            act.wait_ge(sq_done, c - 1)
                        nc.scalar.activation(sq_junk[:], mo_sb[h % 2][:, n - 1, :], ACT.Square,
                                             scale=rden[:, n - 1:n], accum_out=msq[:, n - 1:n]).then_inc(sq_done, 1)
                if kind == "start":
                    take(0)
                    for r in splits_for[3]:
                        hi(r)
                    act.wait_ge(f_ready, 1)
                    step(nc.scalar.activation(rows[3][:], rows[2][:], ACT.Abs))
                    step(nc.scalar.activation(rows[3][:], rows[3][:], ACT.Exp, scale=-1.0))
                    nc.scalar.activation(rows[3][:], rows[3][:], ACT.Ln, bias=1.0).then_inc(log_done, 1)
                    continue
                if kind == "fill" and n == 2:
                    act.wait_ge(f_ready, 2)
                    nc.scalar.activation(srow[:, 5, :], srow[:, 4, :], ACT.Exp).then_inc(dec_exp, 1)
                if kind == "fill" and n == 6:
                    act.wait_ge(bank_free, bank_no[("cols", 3, 1)] + 1)
                    nc.scalar.activation(cols[:, 1:4, :, :], cols[:, 1:4, :, :], ACT.Exp).then_inc(cols_exp, 1)
                for q in waiting:
                    late(q)
                now, waiting = (qs, []) if kind in ("fill", "tail") else (qs[:-1], qs[-1:])
                for q in qs:
                    take(q)
                    if kind == "mlstm" and n and q == qs[-1]:
                        act.wait_ge(pe_keep, keep_no[("A", h, n)] + 1)
                        act.wait_ge(chunk_ready, NT * h + n)
                        nc.scalar.activation(inter[:], keep[:, 0:VE], ACT.Copy, scale=cols[:, 1, n, h:h + 1]
                                             ).then_inc(inter_done, 1)
                    if q in now:
                        late(q)
                    for r in splits_for.get(q + 3, ()):
                        hi(r)
                if kind == "mlstm" and n == NT - 1:
                    act.wait_ge(chunk_ready, NT * (h + 1))
                    act.wait_ge(sq_done, NT * h + n)
                    nc.scalar.activation(sq_junk[:], mo_sb[h % 2][:, n, :], ACT.Square,
                                         scale=rden[:, n:n + 1], accum_out=msq[:, n:n + 1]).then_inc(sq_done, 1)

        @block.vector
        def _(dve):
            steps = [0]

            def step(ins):
                ins.then_inc(v_step, 1)
                steps[0] += 1
                dve.wait_ge(v_step, steps[0])

            V = nc.vector
            TS, TT, STT = V.tensor_scalar, V.tensor_tensor, V.scalar_tensor_tensor

            def rope(q):
                z = quanta[q]
                t = (qa_sb if z.kind == "qa" else ka_sb)[z.head % 2][0:32, z.tile, :]
                d = DIL[z.tile]
                placed = lambda v: v.rearrange("p (r u) -> p r u", r=d)
                table = lambda v: v.rearrange("p (u r) -> p r u", r=d)
                step(V.stream_shuffle(tmp[32:64, :], t, list(range(16, 32)) + list(range(16))))
                step(TT(placed(t), placed(t), table(rope_sb[0:32, :]), ALU.mult))
                step(TT(placed(tmp[0:32, :]), placed(tmp[32:64, :]), table(rope_sb[32:64, :]), ALU.mult))
                TT(t, t, tmp[0:32, :], ALU.add).then_inc(rope_done, 1)
                dve.wait_ge(rope_done, rope_no[q])

            def after(q):
                z = quanta[q]
                slot = tcol(q)
                s = z.head % 2
                if z.kind in BY_ACT:
                    dve.wait_ge(evac, evac_no[q])
                else:
                    dve.wait_ge(pe_quantum, q + 1)
                if z.kind in ("ka", "qa"):
                    rope(q)
                elif z.kind == "za":
                    STT(za_sb[s][:], za_sb[s][:], 1.0, slot, ALU.add, ALU.mult).then_inc(post, 1)
                elif z.kind == "mz":
                    STT(mz_sb[s][:, z.tile, :], mz_sb[s][:, z.tile, :], 1.0, slot, ALU.add, ALU.mult
                        ).then_inc(post, 1)
                elif z.kind == "mv" and z.part == 1:
                    V.memset(mv_sb[s][:, :, MD:VE], 1.0).then_inc(ones_done, 1)
                elif z.kind == "mconv":
                    y = mqk[s][:, z.part, z.tile, :]
                    t = z.part * KT + z.head * 2 + z.tile
                    for d in (1, 2, 3):
                        ins = STT(y[:, d:], slot[:, 0:S - d], cw[:, t, 3 - d:4 - d], y[:, d:], ALU.mult, ALU.add)
                        if d < 3:
                            step(ins)
                    ins.then_inc(post, 1)
                    dve.wait_ge(tanh_done, conv_no[q])
                    STT(y, tmp[:], 1.0, y, ALU.add, ALU.mult).then_inc(silu_done, 1)
                elif z.kind == "pa":
                    g = ga_sb[:, z.tile, :]
                    STT(g, g, 1.0, slot, ALU.add, ALU.mult).then_inc(post, 1)
                elif z.kind == "pm":
                    g, a = gm_sb[:, z.tile, :], ga_sb[:, z.tile, :]
                    STT(g, g, 1.0, slot, ALU.add, ALU.mult).then_inc(post, 1)
                    dve.wait_ge(post, post_no[q])
                    TT(a, a, g, ALU.add).then_inc(sum_done, 1)
                    dve.wait_ge(mg_hi, z.tile + 1)
                    STT(mglo[:, z.tile, :], a, 0.5, mghi[:, z.tile, :].bitcast(F32), ALU.mult, ALU.subtract
                        ).then_inc(mg_lo, 1)

            def gate_rows():
                dve.wait_ge(evac, 1)
                dve.wait_ge(const_in, 16 * NCONST)
                step(V.stream_shuffle(rows[1][:], rows[0][:], [0] * 32))
                step(V.stream_shuffle(rows[2][:], rows[0][:], [1] * 32))
                step(TS(rows[1][:], rows[1][:], bg[:, 0:1], None, ALU.add))
                TS(rows[2][:], rows[2][:], bg[:, 1:2], None, ALU.add).then_inc(f_ready, 1)
                dve.wait_ge(f_ready, 1)
                step(V.memset(rows[8][:], 1.0))
                step(V.memset(rows[9][:], 0.0))
                step(V.memset(rows[8][:, 0:S:P], 0.0))
                step(V.memset(rows[9][:, 0:S:P], NEG))
                dve.wait_ge(log_done, 1)
                step(STT(rows[4][:], rows[2][:], 0.0, rows[3][:], ALU.min, ALU.subtract))
                step(V.tensor_tensor_scan(rows[5][:], rows[8][:], rows[4][:], 0.0, ALU.mult, ALU.add))
                step(TT(rows[6][:], rows[1][:], rows[5][:], ALU.subtract))
                step(V.tensor_tensor_scan(rows[7][:], rows[9][:], rows[6][:], NEG, ALU.add, ALU.max))
                bt, am, mnew, mprev, dk, bm = (srow[:, i, :] for i in (0, 1, 2, 3, 4, 6))
                step(V.tensor_copy(bt, rows[5][:, P - 1:S:P]))
                step(TT(am, bt, rows[7][:, P - 1:S:P], ALU.add))
                step(V.tensor_tensor_scan(mnew, bt, am, 0.0, ALU.add, ALU.max))
                step(V.memset(srow[:, 3, 0:1], 0.0))
                step(V.tensor_copy(srow[:, 3, 1:NT], srow[:, 2, 0:NT - 1]))
                step(TT(bm, bt, mnew, ALU.subtract))
                TT(dk, bm, mprev, ALU.add).then_inc(f_ready, 1)
                each = lambda v: v.unsqueeze(2).broadcast_to([P, NT, P])
                chunked = lambda r: r[:].rearrange("p (j l) -> p j l", l=P)
                step(TT(chunked(rows[7]), chunked(rows[7]), each(mprev), ALU.max))
                step(TS(negg[:], rows[7][:], -1.0, None, ALU.mult))
                step(TT(chunked(rows[0]), chunked(negg), each(mprev), ALU.add))
                step(TT(chunked(rows[3]), chunked(rows[6]), each(bm), ALU.add))
                TT(rows[2][:], negg[:], rows[5][:], ALU.subtract).then_inc(rows_ready, 1)

            def gate_columns():
                for a in range(4):
                    for j2 in range(2):
                        i = bank_no[("cols", a, j2)]
                        dve.wait_ge(pe_bank, i + 1)
                        V.tensor_copy(cols[:, a, 4 * j2:4 * j2 + 4, :],
                                      bank[i % 3][:].rearrange("p (j h x) -> p j h x", j=4, x=32)[:, :, :, 0]
                                      ).then_inc(bank_free, 1)
                i = bank_no[("decay",)]
                dve.wait_ge(pe_bank, i + 1)
                V.tensor_copy(decay[:].rearrange("p h j -> p (h j)"), bank[i % 3][:, 0:MH * NT]
                              ).then_inc(bank_free, 1)

            def head_norm(h):
                dve.wait_ge(sq_done, NT * (h + 1))
                TS(msq[:], msq[:], 1.0 / MD, 4.0 * EPS, ALU.mult, ALU.add).then_inc(m_ms, 1)
                dve.wait_ge(m_rs, h + 1)
                step(TT(mfac[:], mrs[:], rden[:], ALU.mult))
                for j in range(NT):
                    o = mo_sb[h % 2][:, j, :]
                    ins = TS(o, o, mfac[:, j:j + 1], None, ALU.mult)
                ins.then_inc(m_norm, 1)
                dve.wait_ge(m_norm, h + 1)

            def head_gate(h):
                dve.wait_ge(post, post_no[index[("mz", h, 0, 1)]])
                for d in range(2):
                    for j2 in range(2):
                        i = bank_no[("hmT", h, d, j2)]
                        dve.wait_ge(pe_bank, i + 1)
                        z = mz_sb[h % 2][:, d, j2 * 512:(j2 + 1) * 512]
                        STT(z, bank[i % 3][:], mw[:, 2 * h + d:2 * h + d + 1], z, ALU.mult, ALU.mult
                            ).then_inc(bank_free, 1)

            def compare_groups(h):
                dve.wait_ge(ml_in, 16 * NG * (h + 1))
                nm = mlc[:, :, :, 0]
                step(TT(lead[:, 0], nm[:, 0], nm[:, 1], ALU.min))
                step(TT(lead[:, 0], lead[:, 0], nm[:, 2], ALU.min))
                TT(eg[:, 0], lead[:, 0].unsqueeze(1).broadcast_to([NT, NG, P]), nm, ALU.subtract
                   ).then_inc(lead_done, 1)

            def group_shares(h):
                dve.wait_ge(eg_done, h + 1)
                step(TT(eg[:, 1], eg[:, 0], mlc[:, :, :, 1], ALU.mult))
                step(TT(lead[:, 1], eg[:, 1, 0], eg[:, 1, 1], ALU.add))
                step(TT(lead[:, 1], lead[:, 1], eg[:, 1, 2], ALU.add))
                step(V.reciprocal(lead[:, 1], lead[:, 1]))
                TT(eg[:, 2], eg[:, 0], lead[:, 1].unsqueeze(1).broadcast_to([NT, NG, P]), ALU.mult
                   ).then_inc(share_done, 1)

            def combine_groups(h):
                dve.wait_ge(share_in, 16 * (h + 1))
                dve.wait_ge(out_done, NT * (h + 1))
                dve.wait_ge(post, post_no[index[("za", h, 0, 0)]])
                o, z = qa_sb[h % 2], za_sb[h % 2][:]
                by_token = lambda v, d: v.rearrange("p (r u) -> p u r", r=d)
                for g, d in enumerate(DIL):
                    share = share_sb[:, g, :].rearrange("p (u r) -> p u r", r=d)
                    step(TT(share, share, by_token(o[:, g, :], d), ALU.mult))
                step(TT(share_sb[:, 0, :], share_sb[:, 0, :], share_sb[:, 1, :], ALU.add))
                step(TT(share_sb[:, 0, :], share_sb[:, 0, :], share_sb[:, 2, :], ALU.add))
                STT(z, share_sb[:, 0, :], 0.5, z, ALU.mult, ALU.mult).then_inc(att_done, 1)

            dve.wait_ge(start_in, 16 * NSTART)
            dve.wait_ge(g_ready, 2)
            step(V.tensor_copy(raw[:, 0, :, 0:P:32], ifw[:, :, 0:MH]))
            V.tensor_copy(raw[:, 0, :, 1:P:32], ifw[:, :, MH:2 * MH]).then_inc(if_ready, 1)
            for n2 in range(2):
                dve.wait_ge(x_sq, 4 * n2 + 4)
                c = ssq[:, 4 * n2:4 * n2 + 4]
                TS(c, c, 1.0 / DM, EPS, ALU.mult, ALU.add).then_inc(x_ms, 1)
                dve.wait_ge(x_rs, n2 + 1)
                for t in range(4 * n2, 4 * n2 + 4):
                    TS(x_sb[:, t, :], x_sb[:, t, :], ssq[:, NT + t:NT + t + 1], None, ALU.mult).then_inc(x_norm, 1)
            for n2 in range(2):
                for kt in range(KT):
                    i = bank_no[("ht", kt, n2)]
                    dve.wait_ge(ht_hi, i + 1)
                    part = slice(n2 * 512, (n2 + 1) * 512)
                    STT(hlo[:, kt, part], bank[i % 3][:], prew[:, kt:kt + 1], hhi[:, kt, part].bitcast(F32),
                        ALU.mult, ALU.subtract).then_inc(bank_free, 1)
            dve.wait_ge(const_in, 16 * NCONST)
            for part, f in ((0, 0.5), (1, 1.0 / 32.0)):
                tiles = slice(part * KT, (part + 1) * KT)
                step(TS(cw[:, tiles, :], cw[:, tiles, :], f, None, ALU.mult))
                step(TS(cb[:, tiles], cb[:, tiles], f, None, ALU.mult))
            TS(mw[:], mw[:], 0.5, None, ALU.mult).then_inc(cw_ready, 1)
            last_qs = []
            waiting = []
            for kind, h, n, qs in slots:
                if kind == "start":
                    gate_rows()
                    continue
                if kind == "fill" and n == 4:
                    gate_columns()
                if (kind == "mlstm" and h and n == 1) or (kind == "tail" and n == 1):
                    head_gate(h - 1 if kind == "mlstm" else MH - 1)
                if kind == "att":
                    if h >= 2 and n == 0:
                        dve.wait_ge(ml_out, 16 * (h - 1))
                    for g in range(NG):
                        no = bank_no[("score", h, n, g // 2)]
                        dve.wait_ge(pe_bank, no + 1)
                        m, place = key_tiles(g, n), places(n)[g]
                        mask = mask_sb[:, 2 * P:3 * P] if g == 2 else mask_sb[:, (2 - m) * P:2 * P]
                        ins = V.tensor_tensor_reduce(
                            out=prob[:, n % 2, place * P:(place + m) * P],
                            in0=bank[no % 3][:, place % 4 * P:(place % 4 + m) * P], in1=mask,
                            scale=1.0, scalar=-3.0e38, op0=ALU.add, op1=ALU.max, accum_out=pmax[:, g:g + 1])
                        if g:
                            ins.then_inc(bank_free, 1)
                    dve.wait_ge(bank_free, no + 1)
                    TS(ml[:, h % 2, :, n, 0], pmax[:, 0:NG], -ASCALE, None, ALU.mult).then_inc(max_done, 1)
                hp = h - 1 if kind == "att" else AH - 1
                for q in last_qs:
                    z = quanta[q]
                    if z.kind == "va":
                        for j2 in range(2):
                            no = bank_no[("vT", q, j2)]
                            dve.wait_ge(pe_bank, no + 1)
                            V.tensor_copy(va_sb[z.head % 2][:, z.tile, j2 * 512:(j2 + 1) * 512], bank[no % 3][:]
                                          ).then_inc(bank_free, 1)
                last_qs = qs
                if hp >= 0 and (kind == "att" or (kind == "mlstm" and h == 0)):
                    if n == 1:
                        compare_groups(hp)
                    if n == 2:
                        group_shares(hp)
                    if n == 4:
                        combine_groups(hp)
                if kind == "mlstm":
                    c = NT * h + n
                    no = bank_no[("qk", h, n)]
                    dve.wait_ge(pe_bank, no + 1)
                    TT(dmat[:], bank[no % 3][:, P:2 * P], tril[:], ALU.add).then_inc(d_done, 1)
                    dve.wait_ge(e_done, c + 1)
                    TT(wmat[:], bank[no % 3][:, 0:P], emat[:], ALU.mult).then_inc(bank_free, 1)
                for q in waiting:
                    after(q)
                if (kind == "mlstm" and h and n == 0) or (kind == "tail" and n == 0):
                    head_norm(h - 1 if kind == "mlstm" else MH - 1)
                now, waiting = (qs, []) if kind in ("fill", "tail") else (qs[:-1], qs[-1:])
                for q in now:
                    after(q)
                if kind == "att":
                    if NT * h + n >= 2:
                        dve.wait_ge(pe_pv, NT * h + n - 1)
                    for b, (first, w) in enumerate(((0, places(n)[1] + key_tiles(1, n)), (4, 1))):
                        no = bank_no[("probT", h, n, b)]
                        dve.wait_ge(pe_bank, no + 1)
                        V.tensor_copy(probT[:, n % 2, first * P:(first + w) * P], bank[no % 3][:, 0:w * P]
                                      ).then_inc(bank_free, 1)
                if kind == "mlstm":
                    no = bank_no[("B", h, n)]
                    dve.wait_ge(pe_bank, no + 1)
                    if n:
                        dve.wait_ge(inter_done, (NT - 1) * h + n)
                        TT(total[:], inter[:], bank[no % 3][:, 0:VE], ALU.add).then_inc(bank_free, 1)
                    else:
                        V.tensor_copy(total[:], bank[no % 3][:, 0:VE]).then_inc(bank_free, 1)
                    dve.wait_ge(bank_free, no + 1)
                    dl = total[:, MD:VE]
                    step(STT(den[:, 0:1], dl, -1.0, dl, ALU.mult, ALU.max))
                    step(TT(den[:, 1:2], den[:, 0:1], cols[:, 3, n, h:h + 1], ALU.max))
                    step(V.reciprocal(rden[:, n:n + 1], den[:, 1:2]))
                    if n == 0:
                        dve.wait_ge(evac, evac_no[index[("mo", h, 1, 0)]])
                    o = mo_sb[h % 2][:, n, :]
                    STT(o, o, 1.0, total[:, 0:MD], ALU.add, ALU.mult).then_inc(chunk_ready, 1)
                    dve.wait_ge(chunk_ready, NT * h + n + 1)
                    if n < NT - 1:
                        for d in range(2):
                            no = bank_no[("C", h, n, d)]
                            dve.wait_ge(pe_bank, no + 1)
                            if n:
                                STT(state[:, d, :], state[:, d, :], decay[:, h, n:n + 1], bank[no % 3][:, 0:VE],
                                    ALU.mult, ALU.add).then_inc(bank_free, 1)
                            else:
                                V.tensor_copy(state[:, d, :], bank[no % 3][:, 0:VE]).then_inc(bank_free, 1)
            dve.wait_ge(x2_in, 32)
            for i in range(2):
                dve.wait_ge(sq_done, MH * NT + 4 * (7 + i))
                step(V.tensor_reduce(ysum[:, 4 * i:4 * i + 4], ysq[:, 4 * i:4 * i + 4, :], AX.X, ALU.add))
                TS(ysum[:, 4 * i:4 * i + 4], ysum[:, 4 * i:4 * i + 4], 1.0 / DM, EPS, ALU.mult, ALU.add
                   ).then_inc(y_ms, 1)
                dve.wait_ge(y_rs, i + 1)
                for t in range(4 * i, 4 * i + 4):
                    step(STT(y_sb[:, t, :], y_sb[:, t, :], yrs[:, t:t + 1], pw_sb[:], ALU.mult, ALU.mult))
                    TT(y_sb[:, t, :], y_sb[:, t, :], x2_sb[:, t, :], ALU.add).then_inc(y_done, 1)


def constants():
    i = np.arange(P)
    query, key = i[:, None], i[None, :]
    residue = S // DIL[2]
    seen = np.concatenate([key >= query, key <= query,
                           (key <= query) & (key // residue == query // residue)], axis=1)
    mask = np.where(seen, 0.0, NEG).astype(np.float32)
    tril = np.where(i[:, None] <= i[None, :], 0.0, NEG).astype(np.float32)
    half = AD // 8
    freq = np.float32(500000.0) ** (-np.arange(0, 2 * half, 2, dtype=np.float32) / np.float32(2 * half))
    ang = (np.arange(S, dtype=np.float32)[:, None] * freq[None, :].astype(np.float32)).astype(np.float32)
    cos, sin = np.cos(ang).T, np.sin(ang).T
    rope = np.concatenate([cos, cos, -sin, sin]).astype(np.float32)
    return np.eye(P, dtype=np.float32), (mask.view(np.uint32) >> 16).astype(np.uint16), tril, rope


def kernel(x, pre_norm_w, w_in, b_if, conv_w, conv_b, m_norm_w, w_proj_m, w_proj_a, w_out, post_norm_w):
    import concourse.bacc as bacc
    from concourse.bass_utils import run_bass_kernel_spmd

    a = np.ascontiguousarray
    by_tile = lambda v: a(np.asarray(v).reshape(-1, P).T)
    eye, mask, tril, rope = constants()
    b = np.asarray(b_if)[0]
    arrays = {
        "x_in": a(np.asarray(x)[0]),
        "w_in": a(np.asarray(w_in)[0]),
        "w_pm": a(np.asarray(w_proj_m)[0]),
        "w_pa": a(np.asarray(w_proj_a)[0]),
        "w_out": a(np.asarray(w_out)[0]),
        "b_gate": a(np.stack([np.repeat(b[:MH], 32), np.repeat(b[MH:], 32)], 1)),
        "conv_wt": a(np.asarray(conv_w)[0].reshape(4, 16, P).transpose(2, 1, 0)),
        "conv_bt": by_tile(np.asarray(conv_b)[0]),
        "pre_wt": by_tile(np.asarray(pre_norm_w)[0]),
        "m_wt": by_tile(np.asarray(m_norm_w)[0]),
        "post_w": a(np.asarray(post_norm_w)[0]),
        "c_ident": eye, "c_mask": mask, "c_tril": tril, "c_rope": rope,
    }
    nc = bacc.Bacc("TRN2", target_bir_lowering=False, num_devices=1, dynamic_dma_scratch_size=1024)
    args = [nc.dram_tensor(n, v.shape, mybir.dt.from_np(v.dtype), kind="ExternalInput").ap()
            for n, v in arrays.items()]
    args.append(nc.dram_tensor("out", (S, DM), F32, kind="ExternalOutput").ap())
    hybrid_kernel(nc, *args)
    r = run_bass_kernel_spmd(nc, [arrays], core_ids=[0])
    return r.results[0]["out"].reshape(1, S, DM)
```

```python
from contextlib import ExitStack

import numpy as np

import concourse.bass as bass
from concourse import mybir
from concourse.alu_op_type import AluOpType as ALU

ACT = mybir.ActivationFunctionType
AX = mybir.AxisListType
F32 = mybir.dt.float32
F32R = mybir.dt.float32r
BF16 = mybir.dt.bfloat16

P = 128
DM = 1024
S = 1024
KT = DM // P
NT = S // P
MH, MD = 4, 256
AH, AD, NG = 4, 128, 3
AOUT = AH * AD
GROUPS = ((128, 1), (512, 4), (2048, 16))
DIL = [d for _, d in GROUPS]
assert all(w // d == P for w, d in GROUPS)
EPS = 1e-6
NEG = -1.0e30
ASCALE = float(AD) ** -0.5
C_QM, C_KM, C_VM, C_OM, C_ZM = (i * DM for i in range(5))
C_IF = 5 * DM
C_QA = C_IF + 2 * MH
C_KA = C_QA + NG * AOUT
C_VA = C_KA + NG * AOUT
C_ZA = C_VA + NG * AOUT
C_GM = C_ZA + AOUT
C_GA = C_GM + DM

SLOT_QUANTA = (1, 1, 1, 2, 1, 1, 1, 2)
WSLOTS = 4
Y_ORDER = ((0, 0), (0, 1), (1, 0), (1, 1), (2, 0), (3, 0), (2, 1), (3, 1))


class Quantum:

    def __init__(self, kind, form, head=0, part=0, tile=0, width=128):
        self.kind, self.form = kind, form
        self.head, self.part, self.tile, self.width = head, part, tile, width


def att_quanta(h):
    out = [Quantum(kind, "T", h, tile=g) for kind in ("va", "ka", "qa") for g in range(NG)]
    return out + [Quantum("za", "T", h)]


def mlstm_quanta(h):
    out = [Quantum("mconv", "T", h, part=p, tile=d) for p in range(2) for d in range(2)]
    out += [Quantum("mo", "N", h, part=i, width=256) for i in range(2)]
    out += [Quantum("mv", "N", h, part=i, width=256) for i in range(2)]
    return out + [Quantum("mz", "T", h, tile=d) for d in range(2)]


def plan():
    quanta, slots = [Quantum("if", "T")], [("start", 0, 0, [0])]

    def take(new):
        first = len(quanta)
        quanta.extend(new)
        return list(range(first, len(quanta)))

    slots += [("fill", 0, i, [q]) for i, q in enumerate(take(att_quanta(0)))]
    gates = [Quantum("gate", "T", tile=t, part=p) for p in range(2) for t in range(KT)]
    for name, count in (("att", AH), ("mlstm", MH)):
        for h in range(count):
            if h + 1 < count:
                new = att_quanta(h + 1) if name == "att" else mlstm_quanta(h + 1)
            else:
                new = mlstm_quanta(0) if name == "att" else gates[:10]
            ids = take(new)
            at = 0
            for n, k in enumerate(SLOT_QUANTA):
                slots.append((name, h, n, ids[at:at + k]))
                at += k
    tail = take(gates[10:] + [Quantum("pa", "T", tile=t) for t in range(KT)]
                + [Quantum("pm", "T", tile=t) for t in range(KT)]
                + [Quantum("y", "N", tile=c, part=i, width=256) for c, i in Y_ORDER])
    slots += [("tail", 0, i, [q]) for i, q in enumerate(tail)]
    return quanta, slots



def key_tiles(g, n):
    per_residue = S // DIL[g] // P
    return 2 if per_residue > 1 and n % per_residue else 1


def places(n):
    return (0, key_tiles(0, n), 4)


def att_tiles(kind, h, n):
    if (kind, h, n) == ("mlstm", 0, 0):
        return [(1, AH - 1, NT - 1), (2, AH - 1, NT - 2), (2, AH - 1, NT - 1)]
    if kind != "att":
        return []
    return [(back, *divmod(NT * h + n - back, NT)) for back in (1, 2) if NT * h + n >= back]


def hybrid_kernel(nc, x, w_in, w_pm, w_pa, w_out, b_gate, conv_wt, conv_bt, pre_wt, m_wt, post_w,
                  c_ident, c_mask, c_tril, c_rope, out):
    quanta, slots = plan()
    NQ = len(quanta)
    index = {(q.kind, q.head, q.part, q.tile): i for i, q in enumerate(quanta)}
    FIRST_PA = index[("pa", 0, 0, 0)]
    FIRST_PM = index[("pm", 0, 0, 0)]
    FIRST_Y = index[("y", 0, 0, 0)]

    loads = []
    splits_for = {}
    need = {}
    for q in range(NQ):
        mine = []
        if q == FIRST_PA - 1:
            mine += [("att", t) for t in range(AH)]
        if FIRST_PA + 3 <= q < FIRST_PM - 1:
            t = 2 * (q - FIRST_PA - 3)
            mine += [("hm", t), ("hm", t + 1)]
        mine.append(("w", q))
        splits_for[q] = range(len(loads), len(loads) + len(mine))
        loads += mine
    for q in range(NQ):
        last = q + 1 if quanta[q].width == 256 and quanta[q].part == 0 else q
        if quanta[q].kind == "y":
            last = FIRST_Y + 2 * quanta[q].tile + 1
        need[q] = splits_for[last][-1] + 1
    def by_pool(r):
        return loads[r][0] == "w" and r > 0

    pool_lo = [sum(by_pool(i) for i in range(r)) for r in range(len(loads) + 1)]
    dve_lo = [r - n for r, n in enumerate(pool_lo)]

    def split_after(q):
        if q == FIRST_Y + 3:
            return [*splits_for[q + 3], *splits_for[q + 4]]
        return splits_for[q + 3] if q < FIRST_Y + 3 else ()

    def wslot(q):
        return (q - 1) % WSLOTS

    def chunk_done(q):
        return 1 if q == 0 else 2 * ((q - 1) // 2) + 3

    BY_ACT = {"if", "va", "ka", "qa", "za", "mconv", "mv", "mo", "mz", "gate"}
    BY_DVE = {"za", "mconv", "mz", "pa", "pm", "y"}
    evac_no, post_no = {}, {}
    for i, q in enumerate(quanta):
        evac_no[i] = sum(z.kind in BY_ACT for z in quanta[:i + 1])
        post_no[i] = sum((z.kind in BY_DVE) + (z.kind == "y") for z in quanta[:i + 1])
    rope_no = {i: sum(z.kind in ("ka", "qa") for z in quanta[:i + 1]) for i in range(NQ)}
    conv_no = {i: sum(z.kind == "mconv" for z in quanta[:i + 1]) for i in range(NQ)}

    bank_no, keep_no = {}, {}

    def number(table, key):
        table[key] = len(table)

    ht_order = [(kt, 0) for kt in range(3)]
    for kt in range(KT):
        ht_order += [(kt, 1)] + ([(kt + 3, 0)] if kt + 3 < KT else [])
    ht_free = {k: i for i, k in enumerate(ht_order)}
    for i in range(2 * KT):
        number(bank_no, ("ht", i))
    last_qs = []
    for kind, h, n, qs in slots:
        for back, ht, nt in att_tiles(kind, h, n):
            if back == 1:
                number(bank_no, ("probT", ht, nt, 0))
                number(bank_no, ("probT", ht, nt, 1))
        if kind == "att":
            number(bank_no, ("score", h, n, 0))
            number(bank_no, ("score", h, n, 1))
        if kind == "fill" and n == 3:
            for a in range(4):
                for j2 in range(2):
                    number(bank_no, ("cols", a, j2))
            number(bank_no, ("decay",))
        for q in last_qs:
            if quanta[q].kind == "va":
                number(bank_no, ("vT", q, 0))
                number(bank_no, ("vT", q, 1))
        last_qs = qs
        if (kind == "mlstm" and h and n == 1) or (kind == "tail" and n == 1):
            hp = h - 1 if kind == "mlstm" else MH - 1
            for d in range(2):
                for j2 in range(2):
                    number(bank_no, ("hmT", hp, d, j2))
        if kind == "mlstm":
            number(bank_no, ("qk", h, n))
            if n < NT - 1:
                number(keep_no, ("k", h, n))
            if n:
                number(keep_no, ("A", h, n))
            number(bank_no, ("B", h, n))
            if n < NT - 1:
                number(bank_no, ("C", h, n, 0))
                number(bank_no, ("C", h, n, 1))

    ctx = ExitStack()
    with ctx:
        at0 = (nc.sbuf_base + 63) // 64 * 64
        A_H = at0
        A_W = A_H + 2 * KT * S * 4
        A_D = A_W + (2 + 2 * WSLOTS) * 4096
        VE = MD + 1
        SET = (4 * 8192 + NT * VE * 4 + 63) // 64 * 64
        A_E = A_D + 2 * SET

        def at(name, shape, dt, offset):
            return nc.alloc_sbuf_tensor_at(name, shape, dt, offset=offset)

        hhi = at("hhi", [P, KT, S], F32R, A_H)
        hlo = at("hlo", [P, KT, S], F32R, A_H + KT * S * 4)
        raw = at("raw", [P, 2, KT, P], F32, A_W)
        whi = at("whi", [P, WSLOTS, KT, P], F32R, A_W + 2 * 4096)
        wlo = at("wlo", [P, WSLOTS, KT, P], F32R, A_W + (2 + WSLOTS) * 4096)

        ka_sb, va_sb, qa_sb, za_sb, mqk, mv_sb, mo_sb, mz_sb = [], [], [], [], [], [], [], []
        for i in range(2):
            b = A_D + i * SET
            ka_sb.append(at(f"ka{i}", [P, NG, S], F32, b))
            va_sb.append(at(f"va{i}", [P, NG, S], F32, b + NG * 4096))
            qa_sb.append(at(f"qa{i}", [P, NG, S], F32, b + 2 * NG * 4096))
            za_sb.append(at(f"za{i}", [P, S], F32, b + 3 * NG * 4096))
            mqk.append(at(f"mqk{i}", [P, 2, 2, S], F32, b))
            mo_sb.append(at(f"mo{i}", [P, NT, MD], F32, b + 16384))
            mv_sb.append(at(f"mv{i}", [P, NT, VE], F32, b + 24576))
            mz_sb.append(at(f"mz{i}", [P, 2, S], F32, b + SET - 8192))
        x_sb = at("x_sb", [P, NT, DM], F32, A_D)
        rows = [at(f"row{i}", [P, S], F32, A_D + SET + i * 4096) for i in range(10)]
        gm_sb = at("gm_sb", [P, KT, S], F32, A_D)
        ga_sb = at("ga_sb", [P, KT, S], F32, A_D + KT * 4096)
        mghi = at("mghi", [P, KT, S], F32R, A_D)
        mglo = at("mglo", [P, KT, S], F32R, A_D + KT * 4096)
        athi = at("athi", [P, AH, S], F32R, A_D + 2 * KT * 4096)
        atlo = at("atlo", [P, AH, S], F32R, A_D + 2 * KT * 4096 + AH * 4096)
        hmhi = at("hmhi", [P, KT, S], F32R, A_H)
        hmlo = at("hmlo", [P, KT, S], F32R, A_H + KT * S * 4)
        y_sb = at("y_sb", [P, NT, DM], F32, A_H)
        x2_sb = at("x2_sb", [P, NT, DM], F32, A_H + NT * DM * 4)
        pw_sb = at("pw_sb", [P, DM], F32, A_D + 2 * KT * 4096)

        pos = [A_E]

        def small(name, shape, dt, size=4):
            t = at(name, shape, dt, pos[0])
            pos[0] += (int(np.prod(shape[1:])) * size + 31) // 32 * 32
            return t

        rope_sb = small("rope_sb", [64, S], F32)
        share_sb = small("share_sb", [P, NG, S], F32)
        assert A_D + 2 * KT * 4096 + 2 * AH * 4096 <= pos[0]
        mask_sb = small("mask_sb", [P, 3 * P], BF16, 2)
        A_M = pos[0]
        prob = small("prob", [P, 2, 5 * P], F32)
        probT = small("probT", [P, 2, 5 * P], F32)
        ml = small("ml", [P, 2, NG, NT, 2], F32)
        mlc = at("mlc", [NT, NG, P, 2], F32, A_E + 4096)
        lead = at("lead", [NT, 2, P], F32, A_E + 4096 + 3072)
        eg = at("eg", [NT, 3, NG, P], F32, A_E + 4096 + 4096)
        tmp = small("tmp", [P, S], F32)
        ident = small("ident", [P, P], F32)
        tril = small("tril", [P, P], F32)
        cols = small("cols", [P, 4, NT, MH], F32)
        decay = small("decay", [P, MH, NT], F32)
        cw = small("cw", [P, 16, 4], F32)
        cb = small("cb", [P, 16], F32)
        prew = small("prew", [P, KT], F32)
        mw = small("mw", [P, KT], F32)
        bg = small("bg", [P, 2], F32)
        ifw = small("ifw", [P, KT, 2 * MH], F32)
        srow = small("srow", [P, 8, NT], F32)
        halfneg = small("halfneg", [P, NT], F32)
        ssq = small("ssq", [P, 2 * NT], F32)
        pmax = small("pmax", [P, 8], F32)
        den = small("den", [P, 2], F32)
        rden = small("rden", [P, NT], F32)
        msq = small("msq", [P, NT], F32)
        mrs = small("mrs", [P, NT], F32)
        ysq = small("ysq", [P, NT, 4], F32)
        ysum = small("ysum", [P, NT], F32)
        yrs = small("yrs", [P, NT], F32)
        junk = tmp
        mfac = small("mfac", [P, NT], F32)
        neg_g = [at(f"neg_g{i}", [P, S], F32, A_E + i * 4096) for i in range(2)]
        end, pos[0] = pos[0], A_M
        state = small("state", [P, 2, VE], F32)
        kw = small("kw", [P, MD], F32)
        dmat = small("dmat", [P, P], F32)
        emat = small("emat", [P, P], F32)
        wmat = small("wmat", [P, P], F32)
        inter = small("inter", [P, VE], F32)
        total = small("total", [P, VE], F32)
        sq_junk = small("sq_junk", [P, MD], F32)
        assert pos[0] <= A_M + 2 * 2 * 5 * P * 4
        pos[0] = end
        assert pos[0] <= nc.sbuf_usable_end, (pos[0], nc.sbuf_usable_end)

        proj = ctx.enter_context(nc.psum_tensor("proj", [P, 2, 1024], F32))
        bank = [ctx.enter_context(nc.psum_tensor(f"bank{i}", [P, 512], F32)) for i in range(3)]
        keep = ctx.enter_context(nc.psum_tensor("keep", [P, 512], F32))
        ht_bank = [proj[:, i // 2, i % 2 * 512:(i % 2 + 1) * 512] for i in range(4)] + [b[:] for b in bank] + [keep[:]]

        att_dram = nc.dram_tensor("att_spill", [AOUT, S], F32).ap()
        hm_dram = nc.dram_tensor("hm_spill", [DM, S], F32).ap()
        g_dram = nc.dram_tensor("g_spill", [MH, S], F32).ap()
        ml_dram = nc.dram_tensor("ml_spill", [AH, NG, S, 2], F32).ap()
        share_dram = nc.dram_tensor("share_spill", [AH, NG, S], F32).ap()

        def sem(name):
            return ctx.enter_context(nc.semaphore(name))

        x_in = [sem(f"x_in{i}") for i in range(NT)]
        start_in = sem("start_in")
        const_in = sem("const_in")
        NSTART, NCONST = 3, 7
        raw_in = [sem(f"raw_in{i}") for i in range(2)]
        att_out = sem("att_out")
        hm_out = sem("hm_out")
        g_out = sem("g_out")
        g_in = sem("g_in")
        ml_out = sem("ml_out")
        ml_in = sem("ml_in")
        share_out = sem("share_out")
        share_in = sem("share_in")
        pw_in = sem("pw_in")
        x2_in = sem("x2_in")
        y_out = sem("y_out")
        pe_quantum = sem("pe_quantum")
        pe_ybank = sem("pe_ybank")
        pe_bank = sem("pe_bank")
        pe_keep = sem("pe_keep")
        pe_pv = sem("pe_pv")
        hi_done = sem("hi_done")
        ht_hi = sem("ht_hi")
        evac = sem("evac")
        a_step = sem("a_step")
        x_sq = sem("x_sq")
        log_done = sem("log_done")
        dec_exp = sem("dec_exp")
        cols_exp = sem("cols_exp")
        p_exp = sem("p_exp")
        out_done = sem("out_done")
        eg_done = sem("eg_done")
        tanh_done = sem("tanh_done")
        kw_done = sem("kw_done")
        inter_done = sem("inter_done")
        e_done = sem("e_done")
        sq_done = sem("sq_done")
        mg_hi = sem("mg_hi")
        v_step = sem("v_step")
        if_ready = sem("if_ready")
        x_ms = sem("x_ms")
        x_norm = sem("x_norm")
        bank_free = sem("bank_free")
        f_ready = sem("f_ready")
        rows_ready = sem("rows_ready")
        post = sem("post")
        rope_done = sem("rope_done")
        silu_done = sem("silu_done")
        max_done = sem("max_done")
        lead_done = sem("lead_done")
        share_done = sem("share_done")
        att_done = sem("att_done")
        d_done = sem("d_done")
        cw_ready = sem("cw_ready")
        ones_done = sem("ones_done")
        chunk_ready = sem("chunk_ready")
        m_ms = sem("m_ms")
        m_norm = sem("m_norm")
        sum_done = sem("sum_done")
        mg_lo = sem("mg_lo")
        y_ms = sem("y_ms")
        y_done = sem("y_done")
        vlo_done = sem("vlo_done")
        lo_done = sem("lo_done")
        g_ready = sem("g_ready")
        x_rs = sem("x_rs")
        m_rs = sem("m_rs")
        y_rs = sem("y_rs")

        block = ctx.enter_context(nc.Block())

        def tcol(t):
            return proj[:, t % 2, :]

        @block.sync
        def _(sp):
            for t in range(NT):
                if t == 1:
                    sp.dma_start(ident[:], c_ident).then_inc(start_in, 16)
                    sp.dma_start(prew[:], pre_wt).then_inc(start_in, 16)
                    sp.dma_start(ifw[:], w_in[:, C_IF:C_IF + 2 * MH].rearrange("(k p) c -> p k c", p=P)
                                 ).then_inc(start_in, 16)
                sp.dma_start(x_sb[:, t, :], x[t * P:(t + 1) * P, :]).then_inc(x_in[t], 16)
            for dst, src in ((bg, b_gate), (cw, conv_wt), (cb, conv_bt), (mw, m_wt), (tril, c_tril),
                             (mask_sb, c_mask), (rope_sb, c_rope)):
                into = dst[:].bitcast(mybir.dt.uint16) if dst is mask_sb else dst[:]
                sp.dma_start(into, src).then_inc(const_in, 16)

            def columns(q):
                z = quanta[q]
                h, p, t = z.head, z.part, z.tile
                if z.kind in ("qa", "ka", "va"):
                    return w_in, {"qa": C_QA, "ka": C_KA, "va": C_VA}[z.kind] + t * AOUT + h * AD
                if z.kind == "za":
                    return w_in, C_ZA + h * AD
                if z.kind == "mconv":
                    return w_in, (C_QM, C_KM)[p] + h * MD + t * P
                if z.kind in ("mv", "mo"):
                    return w_in, (C_VM if z.kind == "mv" else C_OM) + h * MD + p * P
                if z.kind == "mz":
                    return w_in, C_ZM + h * MD + t * P
                if z.kind == "gate":
                    return w_in, (C_GM, C_GA)[p] + t * P
                if z.kind == "pa":
                    return w_pa, t * P
                if z.kind == "pm":
                    return w_pm, t * P
                return w_out, (q - FIRST_Y) * P

            def att_exchange(h, at):
                if at == 3:
                    sp.wait_ge(p_exp, NG * NT * (h + 1))
                    sp.dma_start(ml_dram[h].rearrange("g (n p) c -> p (g n) c", p=P),
                                 ml[:, h % 2].rearrange("p g n c -> p (g n) c")).then_inc(ml_out, 16)
                if at == 4:
                    sp.wait_ge(ml_out, 16 * (h + 1))
                    if h:
                        sp.wait_ge(att_done, h)
                    for g, d in enumerate(DIL):
                        sp.dma_start(mlc[:, g].rearrange("t (l r) c -> t l r c", r=d),
                                     ml_dram[h, g].rearrange("(r t l) c -> t l r c", r=d, t=NT)
                                     ).then_inc(ml_in, 16)
                if at == 7:
                    sp.wait_ge(share_done, h + 1)
                    sp.dma_start(share_dram[h].rearrange("g (t l) -> t g l", t=NT), eg[:, 2]
                                 ).then_inc(share_out, 16)
                if at == 8:
                    sp.wait_ge(share_out, 16 * (h + 1))
                    sp.dma_start(share_sb[:].rearrange("p g s -> p (g s)"),
                                 share_dram[h].rearrange("g s -> (g s)").partition_broadcast(P)
                                 ).then_inc(share_in, 16)

            for r, (what, i) in enumerate(loads):
                if r == 0:
                    continue
                if what == "w":
                    for h in range(AH):
                        first = index[("va", h + 2, 0, 0)] if h < AH - 2 else index[("mconv", h - AH + 2, 0, 0)]
                        att_exchange(h, i - first)
                        if i == first + 10:
                            sp.wait_ge(att_done, h + 1)
                            sp.dma_start(att_dram[h * P:(h + 1) * P, :], za_sb[h % 2][:]
                                         ).then_inc(att_out, 16)
                    for h in range(MH):
                        mark = index[("mo", h + 2, 0, 0)] if h < MH - 2 else (
                            index[("gate", 0, 0, 4)] if h == MH - 2 else FIRST_PA - 2)
                        if i == mark:
                            sp.wait_ge(bank_free, bank_no[("hmT", h, 1, 1)] + 1)
                            sp.dma_start(hm_dram[h * MD:(h + 1) * MD, :].rearrange("(d p) s -> p d s", p=P),
                                         mz_sb[h % 2][:]).then_inc(hm_out, 16)
                if what == "w" and i == index[("za", 0, 0, 0)]:
                    sp.wait_ge(rows_ready, 1)
                    sp.dma_start(g_dram, rows[8][0:P:32, :]).then_inc(g_out, 16)
                for h in range(MH):
                    if what == "w" and i == (index[("mconv", h + 1, 0, 0)] if h < MH - 1 else index[("gate", 0, 0, 0)]):
                        if h == 0:
                            sp.wait_ge(g_out, 16)
                            sp.wait_ge(rope_done, rope_no[NQ - 1])
                        if h == 1:
                            sp.wait_ge(att_done, AH)
                        if h >= 2:
                            sp.wait_ge(d_done, NT * (h - 1))
                        sp.dma_start(neg_g[h % 2][:], g_dram[h].partition_broadcast(P)).then_inc(g_in, 16)
                if what == "w" and i == FIRST_PM + 4:
                    sp.wait_ge(pe_quantum, FIRST_PM)
                    sp.dma_start(pw_sb[:], post_w.partition_broadcast(P)).then_inc(pw_in, 16)
                if what == "w" and i == FIRST_Y + 5:
                    sp.wait_ge(pe_quantum, FIRST_Y)
                    sp.dma_start(x2_sb[:], x.rearrange("(t p) d -> p t d", p=P)).then_inc(x2_in, 16)
                slot = r % 2
                if r >= 2:
                    sp.wait_ge(hi_done, r - 1)
                    if by_pool(r - 2):
                        sp.wait_ge(lo_done, pool_lo[r - 1])
                    else:
                        sp.wait_ge(vlo_done, dve_lo[r - 1])
                if what == "w":
                    src, c = columns(i)
                    k = src.shape[0] // P
                    sp.dma_start(raw[:, slot, 0:k, :], src[:, c:c + P].rearrange("(k p) c -> p k c", p=P)
                                 ).then_inc(raw_in[slot], 16)
                else:
                    if what == "att":
                        sp.wait_ge(att_out, 16 * AH)
                        src = att_dram
                    else:
                        sp.wait_ge(hm_out, 16 * MH)
                        src = hm_dram
                    sp.dma_start(raw[:, slot, :, :].rearrange("p k c -> p (k c)"), src[i * P:(i + 1) * P, :]
                                 ).then_inc(raw_in[slot], 16)
            for t in range(NT):
                sp.wait_ge(y_done, t + 1)
                sp.dma_start(out[t * P:(t + 1) * P, :], y_sb[:, t, :]).then_inc(y_out, 16)
            sp.wait_ge(y_out, 16 * NT)

        def raw_wait(eng, r):
            if r == 0:
                eng.wait_ge(if_ready, 1)
            else:
                slot = r % 2
                eng.wait_ge(raw_in[slot], 16 * (r // 2 + (1 if slot else 0)))

        def split_views(r):
            what, i = loads[r]
            src = raw[:, r % 2, :, :]
            if what == "w":
                k = AH if quanta[i].kind == "pa" else KT
                return src[:, 0:k, :], whi[:, wslot(i), 0:k, :], wlo[:, wslot(i), 0:k, :]
            flat = src.rearrange("p k c -> p (k c)")
            return (flat, athi[:, i, :], atlo[:, i, :]) if what == "att" else (flat, hmhi[:, i, :], hmlo[:, i, :])

        def split_target_wait(eng, r):
            what, i = loads[r]
            if what == "w":
                if i >= WSLOTS:
                    eng.wait_ge(pe_quantum, chunk_done(i - WSLOTS))
            elif what == "att":
                eng.wait_ge(hm_out, 16 * MH)
            else:
                eng.wait_ge(pe_quantum, FIRST_PA)

        @block.gpsimd
        def _(g):
            nc.gpsimd.memset(raw[:, 0, :, :], 0.0).then_inc(g_ready, 1)
            nc.gpsimd.memset(halfneg[:], -0.5).then_inc(g_ready, 1)

            def lo(r):
                src, hi, low = split_views(r)
                raw_wait(g, r)
                if by_pool(r):
                    g.wait_ge(hi_done, r + 1)
                    nc.gpsimd.tensor_tensor(low, src, hi.bitcast(F32), ALU.subtract).then_inc(lo_done, 1)

            g.wait_ge(g_ready, 2)
            for t in range(NT):
                g.wait_ge(x_ms, t + 1)
                nc.gpsimd.tensor_tensor(ssq[:, NT + t:NT + t + 1], ssq[:, t:t + 1], halfneg[:, 0:1], ALU.pow
                                        ).then_inc(x_rs, 1)
            for q in range(3):
                for r in splits_for[q]:
                    lo(r)
            for kind, h, n, qs in slots:
                if (kind == "mlstm" and h and n == 0) or (kind == "tail" and n == 0):
                    hp = h - 1 if kind == "mlstm" else MH - 1
                    g.wait_ge(m_ms, hp + 1)
                    nc.gpsimd.tensor_tensor(mrs[:], msq[:], halfneg[:], ALU.pow).then_inc(m_rs, 1)
                for q in qs:
                    for r in split_after(q):
                        lo(r)
            for i in range(NT // 2):
                g.wait_ge(y_ms, i + 1)
                nc.gpsimd.tensor_tensor(yrs[:, 2 * i:2 * i + 2], ysum[:, 2 * i:2 * i + 2], halfneg[:, 0:2], ALU.pow
                                        ).then_inc(y_rs, 1)

        @block.tensor
        def _(pe):
            fills = [0]

            def work(key):
                i = bank_no[key]
                assert i == fills[0]
                fills[0] += 1
                if i >= 3:
                    pe.wait_ge(bank_free, i - 2)
                return bank[i % 3]

            def quantum(q):
                z = quanta[q]
                pe.wait_ge(lo_done, pool_lo[need[q]])
                pe.wait_ge(vlo_done, dve_lo[need[q]])
                if q >= 2:
                    if quanta[q - 2].kind == "y":
                        pe.wait_ge(sq_done, MH * NT + 4 * (q - 1 - FIRST_Y))
                    if quanta[q - 2].kind in BY_DVE:
                        pe.wait_ge(post, post_no[q - 2])
                    else:
                        pe.wait_ge(evac, evac_no[q - 2])
                ws = wslot(q)
                slot = tcol(q)
                if z.form == "T":
                    mhi, mlo, k = hhi, hlo, KT
                    if z.kind == "pa":
                        mhi, mlo, k = athi, atlo, AH
                    if z.kind == "pm":
                        mhi, mlo = hmhi, hmlo
                    for kt in range(k):
                        for w, m in ((whi, mhi), (whi, mlo), (wlo, mhi)):
                            for half in range(2):
                                mm = pe.matmul(slot[:, half * 512:(half + 1) * 512], w[:, ws, kt, :],
                                               m[:, kt, half * 512:(half + 1) * 512],
                                               start=(kt == 0 and w is whi and m is mhi),
                                               stop=(kt == k - 1 and w is wlo))
                else:
                    shi, slo = (mghi, mglo) if z.kind == "y" else (hhi, hlo)
                    count = 1024 // z.width
                    first = z.part * count if z.width == 256 else 0
                    if z.width == 256:
                        ws = wslot(FIRST_Y + 2 * z.tile if z.kind == "y" else q - z.part)
                    for i in range(count):
                        t = first + i
                        for kt in range(KT):
                            if q == FIRST_Y and i == 0:
                                pe.wait_ge(mg_lo, 2 * kt + 1)
                            if q == FIRST_Y + 1 and i == 0 and kt == 0:
                                pe.wait_ge(mg_lo, 2 * KT)
                            for s, w in ((shi, whi), (shi, wlo), (slo, whi)):
                                rhs = w[:, ws:ws + 2, kt, :] if z.width == 256 else w[:, ws, kt, :]
                                mm = pe.matmul(slot[:, i * z.width:(i + 1) * z.width],
                                               s[:, kt, t * P:(t + 1) * P], rhs,
                                               start=(kt == 0 and s is shi and w is whi),
                                               stop=(kt == KT - 1 and s is slo))
                        if z.kind == "y" and i == 1:
                            mm.then_inc(pe_ybank, 1)
                mm.then_inc(pe_quantum, 1)

            def gate_part(kt):
                for m in (hhi, hlo):
                    for half in range(2):
                        mm = pe.matmul(tcol(0)[:, half * 512:(half + 1) * 512], whi[:, wslot(0), kt, :],
                                       m[:, kt, half * 512:(half + 1) * 512],
                                       start=(kt == 0 and m is hhi), stop=(kt == KT - 1 and m is hlo))
                if kt == KT - 1:
                    mm.then_inc(pe_quantum, 1)

            def scores(h, n):
                pe.wait_ge(rope_done, rope_no[index[("qa", h, 0, NG - 1)]])
                for g in range(NG):
                    if g != 1:
                        b = work(("score", h, n, g // 2))
                    m, place = key_tiles(g, n), places(n)[g] % 4
                    mm = pe.matmul(b[:, place * P:(place + m) * P], qa_sb[h % 2][:, g, n * P:(n + 1) * P],
                                   ka_sb[h % 2][:, g, (n + 1 - m) * P:(n + 1) * P], start=True, stop=True)
                    if g:
                        mm.then_inc(pe_bank, 1)

            def probabilities(h, n):
                pe.wait_ge(p_exp, NG * (NT * h + n + 1))
                count = places(n)[1] + key_tiles(1, n)
                b = work(("probT", h, n, 0))
                for i in range(count):
                    mm = pe.transpose(b[:, i * P:(i + 1) * P], prob[:, n % 2, i * P:(i + 1) * P], ident[:])
                mm.then_inc(pe_bank, 1)
                b = work(("probT", h, n, 1))
                pe.transpose(b[:, 0:P], prob[:, n % 2, 4 * P:5 * P], ident[:]).then_inc(pe_bank, 1)

            def weigh(h, n):
                pe.wait_ge(bank_free, bank_no[("probT", h, n, 1)] + 1)
                if NT * h + n:
                    pe.wait_ge(out_done, NT * h + n)
                for g in range(NG):
                    m, place = key_tiles(g, n), places(n)[g]
                    for i in range(m):
                        k = n + 1 - m + i
                        mm = pe.matmul(keep[:, g * P:(g + 1) * P], va_sb[h % 2][:, g, k * P:(k + 1) * P],
                                       probT[:, n % 2, (place + i) * P:(place + i + 1) * P],
                                       start=(i == 0), stop=(i == m - 1))
                mm.then_inc(pe_pv, 1)

            def turn_values(q):
                z = quanta[q]
                pe.wait_ge(evac, evac_no[q])
                for j2 in range(2):
                    b = work(("vT", q, j2))
                    for i in range(4):
                        t = 4 * j2 + i
                        mm = pe.transpose(b[:, i * P:(i + 1) * P],
                                          ka_sb[z.head % 2][:, z.tile, t * P:(t + 1) * P], ident[:])
                    mm.then_inc(pe_bank, 1)

            def spread(h):
                return ident[:, 32 * h:32 * h + 1].broadcast_to([P, P])

            def keep_wait(i):
                for kind, done in (("k", kw_done), ("A", inter_done)):
                    before = sum(k[0] == kind for k, v in keep_no.items() if v < i)
                    if before:
                        pe.wait_ge(done, before)

            def chunk_start(h, j):
                qk = mqk[h % 2]
                pe.wait_ge(silu_done, conv_no[index[("mconv", h, 1, 1)]])
                if h == 0 and j == 0:
                    pe.wait_ge(out_done, AH * NT)
                tok = slice(j * P, (j + 1) * P)
                b = work(("qk", h, j))
                for d in range(2):
                    mm = pe.matmul(b[:, 0:P], qk[:, 1, d, tok], qk[:, 0, d, tok], start=(d == 0), stop=(d == 1))
                mm.then_inc(pe_bank, 1)
                if j < NT - 1:
                    keep_wait(keep_no[("k", h, j)])
                    for d in range(2):
                        mm = pe.transpose(keep[:, d * P:(d + 1) * P], qk[:, 1, d, tok], ident[:])
                    mm.then_inc(pe_keep, 1)

            def state_part(h, j):
                qk = mqk[h % 2]
                tok = slice(j * P, (j + 1) * P)
                if j:
                    keep_wait(keep_no[("A", h, j)])
                    pe.wait_ge(bank_free, bank_no[("C", h, j - 1, 1)] + 1)
                    for d in range(2):
                        mm = pe.matmul(keep[:, 0:VE], qk[:, 0, d, tok], state[:, d, :],
                                       start=(d == 0), stop=(d == 1))
                    mm.then_inc(pe_keep, 1)

            def chunk_end(h, j):
                v = mv_sb[h % 2]
                pe.wait_ge(bank_free, bank_no[("qk", h, j)] + 1)
                if j == 0:
                    pe.wait_ge(evac, evac_no[index[("mv", h, 1, 0)]])
                    pe.wait_ge(ones_done, h + 1)
                b = work(("B", h, j))
                pe.matmul(b[:, 0:VE], wmat[:], v[:, j, :], start=True, stop=True).then_inc(pe_bank, 1)
                if j < NT - 1:
                    pe.wait_ge(kw_done, (NT - 1) * h + j + 1)
                    for d in range(2):
                        b = work(("C", h, j, d))
                        pe.matmul(b[:, 0:VE], kw[:, d * P:(d + 1) * P], v[:, j, :],
                                  start=True, stop=True).then_inc(pe_bank, 1)

            def head_output(h):
                pe.wait_ge(m_norm, h + 1)
                for d in range(2):
                    for j2 in range(2):
                        b = work(("hmT", h, d, j2))
                        for i in range(4):
                            mm = pe.transpose(b[:, i * P:(i + 1) * P],
                                              mo_sb[h % 2][:, 4 * j2 + i, d * P:(d + 1) * P], ident[:])
                        mm.then_inc(pe_bank, 1)

            pe.wait_ge(start_in, 16 * NSTART)
            for t in range(4):
                pe.wait_ge(x_norm, t + 1)
                for kt in range(KT):
                    mm = pe.transpose(ht_bank[kt][:, t * P:(t + 1) * P], x_sb[:, t, kt * P:(kt + 1) * P], ident[:])
                    if t == 3:
                        mm.then_inc(pe_bank, 1)
            pe.wait_ge(x_norm, NT)
            parts = [(ht_free[kt, 0], 0, kt) for kt in range(KT)]
            parts += [(max(ht_free[kt, 1], ht_free[1, 1]), 1, kt) for kt in range(KT)]
            pe.wait_ge(vlo_done, 1)
            for freed, is_gate, kt in sorted(parts):
                pe.wait_ge(bank_free, freed + 1)
                if is_gate:
                    gate_part(kt)
                    continue
                for i in range(4):
                    mm = pe.transpose(ht_bank[kt][:, i * P:(i + 1) * P],
                                      x_sb[:, 4 + i, kt * P:(kt + 1) * P], ident[:])
                mm.then_inc(pe_bank, 1)
            fills[0] = 2 * KT
            last_qs = []
            for kind, h, n, qs in slots:
                for back, ht, nt in att_tiles(kind, h, n):
                    (probabilities if back == 1 else weigh)(ht, nt)
                if kind == "att":
                    scores(h, n)
                if (kind == "mlstm" and h and n == 1) or (kind == "tail" and n == 1):
                    head_output(h - 1 if kind == "mlstm" else MH - 1)
                if kind == "mlstm":
                    chunk_start(h, n)
                if kind == "fill" and n == 3:
                    pe.wait_ge(rows_ready, 1)
                    for a, r in enumerate((rows[6], rows[0], rows[3], rows[2])):
                        for j2 in range(2):
                            b = work(("cols", a, j2))
                            for i in range(4):
                                j = 4 * j2 + i
                                mm = pe.transpose(b[:, i * P:(i + 1) * P], r[:, j * P:(j + 1) * P], ident[:])
                            mm.then_inc(pe_bank, 1)
                    pe.wait_ge(dec_exp, 1)
                    b = work(("decay",))
                    for hh in range(MH):
                        mm = pe.matmul(b[:, hh * NT:(hh + 1) * NT], spread(hh), srow[:, 5, :],
                                       start=True, stop=True)
                    mm.then_inc(pe_bank, 1)
                for q in qs:
                    if q:
                        quantum(q)
                for q in last_qs:
                    if quanta[q].kind == "va":
                        turn_values(q)
                last_qs = qs
                if kind == "mlstm":
                    state_part(h, n)
                    chunk_end(h, n)

        @block.scalar
        def _(act):
            steps = [0]

            def step(ins):
                ins.then_inc(a_step, 1)
                steps[0] += 1
                act.wait_ge(a_step, steps[0])

            def hi(r):
                src, h, _ = split_views(r)
                raw_wait(act, r)
                split_target_wait(act, r)
                nc.scalar.activation(h, src, ACT.Copy).then_inc(hi_done, 1)

            def take(q):
                z = quanta[q]
                if z.kind == "y":
                    squares(q)
                if z.kind not in BY_ACT:
                    return
                act.wait_ge(pe_quantum, q + 1)
                slot = tcol(q)
                s = z.head % 2
                if z.kind == "if":
                    ins = nc.scalar.activation(rows[0][:], slot, ACT.Copy)
                elif z.kind in ("va", "ka", "qa"):
                    if (z.kind, z.head, z.tile) == ("va", 1, 0):
                        act.wait_ge(g_out, 16)
                    if z.kind == "qa" and z.head >= 2:
                        act.wait_ge(att_done, z.head - 1)
                    dst = (qa_sb if z.kind == "qa" else ka_sb)[s][:, z.tile, :]
                    ins = nc.scalar.activation(dst.rearrange("p (r u) -> p r u", r=DIL[z.tile]),
                                               slot.rearrange("p (u r) -> p r u", r=DIL[z.tile]), ACT.Copy)
                elif z.kind == "za":
                    if z.head >= 2:
                        act.wait_ge(att_out, 16 * (z.head - 1))
                    ins = nc.scalar.activation(za_sb[s][:], slot, ACT.Tanh, scale=0.5)
                elif z.kind == "mconv":
                    t = z.part * KT + z.head * 2 + z.tile
                    act.wait_ge(cw_ready, 1)
                    ins = nc.scalar.activation(mqk[s][:, z.part, z.tile, :], slot, ACT.Identity,
                                               bias=cb[:, t:t + 1], scale=cw[:, t, 3:4])
                elif z.kind == "mv":
                    if z.head < 2:
                        act.wait_ge(att_done, z.head + 3)
                    ins = nc.scalar.activation(mv_sb[s][:, 4 * z.part:4 * z.part + 4, 0:MD],
                                               slot.rearrange("p (n c) -> p n c", c=MD), ACT.Copy)
                elif z.kind == "mo":
                    ins = nc.scalar.activation(mo_sb[s][:, 4 * z.part:4 * z.part + 4, :],
                                               slot.rearrange("p (n c) -> p n c", c=MD), ACT.Tanh, scale=0.5)
                elif z.kind == "mz":
                    if z.head >= 2:
                        act.wait_ge(hm_out, 16 * (z.head - 1))
                    else:
                        act.wait_ge(att_out, 16 * (z.head + 3))
                    ins = nc.scalar.activation(mz_sb[s][:, z.tile, :], slot, ACT.Tanh, scale=0.5)
                elif z.kind == "gate":
                    dst = (gm_sb, ga_sb)[z.part]
                    if z.part == 1 and z.tile == 0:
                        act.wait_ge(hm_out, 16 * (MH - 1))
                    ins = nc.scalar.activation(dst[:, z.tile, :], slot, ACT.Tanh, scale=0.5)
                ins.then_inc(evac, 1)

            def squares(q):
                act.wait_ge(sq_done, MH * NT + 4 * (q - FIRST_Y))
                for i in range(4):
                    if i == 0:
                        act.wait_ge(pe_ybank, q - FIRST_Y + 1)
                    if i == 2:
                        act.wait_ge(pe_quantum, q + 1)
                    t, c = 4 * quanta[q].part + i, quanta[q].tile
                    nc.scalar.activation(junk[:, 256 * i:256 * i + 256], tcol(q)[:, 256 * i:256 * i + 256],
                                         ACT.Square, accum_out=ysq[:, t, c:c + 1]).then_inc(sq_done, 1)

            def output(h, n):
                act.wait_ge(pe_pv, NT * h + n + 1)
                nc.scalar.activation(qa_sb[h % 2][:, :, n * P:(n + 1) * P],
                                     keep[:, 0:NG * P].rearrange("p (g q) -> p g q", q=P), ACT.Copy
                                     ).then_inc(out_done, 1)

            def late(q):
                z = quanta[q]
                if z.kind == "mconv":
                    n = conv_no[q]
                    act.wait_ge(post, post_no[q])
                    if n > 1:
                        act.wait_ge(silu_done, n - 1)
                    nc.scalar.activation(tmp[:], mqk[z.head % 2][:, z.part, z.tile, :], ACT.Tanh,
                                         scale=(1.0, 16.0)[z.part]).then_inc(tanh_done, 1)
                if z.kind == "pm":
                    for i, half in enumerate((slice(0, 512), slice(512, 1024))):
                        act.wait_ge(sum_done, 2 * z.tile + i + 1)
                        nc.scalar.activation(mghi[:, z.tile, half], ga_sb[:, z.tile, half], ACT.Copy,
                                             scale=0.5).then_inc(mg_hi, 1)

            for t in range(NT):
                act.wait_ge(x_in[t], 16)
                if t:
                    act.wait_ge(x_sq, t)
                nc.scalar.activation(junk[:], x_sb[:, t, :], ACT.Square, accum_out=ssq[:, t:t + 1]
                                     ).then_inc(x_sq, 1)
                if t == 4:
                    hi(0)
            act.wait_ge(start_in, 16 * NSTART)
            for i, (kt, n2) in enumerate(ht_order):
                act.wait_ge(pe_bank, n2 * KT + kt + 1)
                nc.scalar.activation(hhi[:, kt, n2 * 512:(n2 + 1) * 512], ht_bank[kt], ACT.Copy,
                                     scale=prew[:, kt:kt + 1]).then_inc(ht_hi, 1)
                if i in (10, 15):
                    for r in splits_for[i // 7]:
                        hi(r)
            waiting = []
            for kind, h, n, qs in slots:
                for back, ht, nt in att_tiles(kind, h, n):
                    if back == 2:
                        output(ht, nt)
                if kind == "att":
                    act.wait_ge(max_done, NT * h + n + 1)
                    for g in range(NG):
                        p = prob[:, n % 2, places(n)[g] * P:(places(n)[g] + key_tiles(g, n)) * P]
                        nc.scalar.activation(p, p, ACT.Exp, bias=ml[:, h % 2, g, n, 0:1], scale=ASCALE,
                                             accum_out=ml[:, h % 2, g, n, 1:2]).then_inc(p_exp, 1)
                if n == 1 and ((kind == "att" and h) or (kind == "mlstm" and h == 0)):
                    act.wait_ge(lead_done, h if kind == "att" else AH)
                    nc.scalar.activation(eg[:, 0], eg[:, 0], ACT.Exp).then_inc(eg_done, 1)
                if kind == "mlstm":
                    c = NT * h + n
                    if n < NT - 1:
                        act.wait_ge(pe_keep, keep_no[("k", h, n)] + 1)
                        if n:
                            act.wait_ge(pe_bank, bank_no[("C", h, n - 1, 1)] + 1)
                        elif h:
                            act.wait_ge(pe_bank, bank_no[("C", h - 1, NT - 2, 1)] + 1)
                        else:
                            act.wait_ge(cols_exp, 1)
                        nc.scalar.activation(kw[:], keep[:, 0:MD], ACT.Copy, scale=cols[:, 2, n, h:h + 1]
                                             ).then_inc(kw_done, 1)
                    act.wait_ge(d_done, c + 1)
                    nc.scalar.activation(emat[:], dmat[:], ACT.Exp, bias=cols[:, 0, n, h:h + 1]
                                         ).then_inc(e_done, 1)
                    if n:
                        act.wait_ge(chunk_ready, c)
                        if c > 1:
                            act.wait_ge(sq_done, c - 1)
                        nc.scalar.activation(sq_junk[:], mo_sb[h % 2][:, n - 1, :], ACT.Square,
                                             scale=rden[:, n - 1:n], accum_out=msq[:, n - 1:n]).then_inc(sq_done, 1)
                if kind == "start":
                    take(0)
                    for r in splits_for[3]:
                        hi(r)
                    act.wait_ge(f_ready, 1)
                    step(nc.scalar.activation(rows[3][:], rows[2][:], ACT.Abs))
                    step(nc.scalar.activation(rows[3][:], rows[3][:], ACT.Exp, scale=-1.0))
                    nc.scalar.activation(rows[3][:], rows[3][:], ACT.Ln, bias=1.0).then_inc(log_done, 1)
                    continue
                if kind == "fill" and n == 2:
                    act.wait_ge(f_ready, 2)
                    nc.scalar.activation(srow[:, 5, :], srow[:, 4, :], ACT.Exp).then_inc(dec_exp, 1)
                if kind == "fill" and n == 6:
                    act.wait_ge(bank_free, bank_no[("cols", 3, 1)] + 1)
                    nc.scalar.activation(cols[:, 1:4, :, :], cols[:, 1:4, :, :], ACT.Exp).then_inc(cols_exp, 1)
                for q in waiting:
                    late(q)
                now, waiting = (qs, []) if kind in ("fill", "tail") else (qs[:-1], qs[-1:])
                for q in qs:
                    take(q)
                    if kind == "mlstm" and n and q == qs[-1]:
                        act.wait_ge(pe_keep, keep_no[("A", h, n)] + 1)
                        act.wait_ge(chunk_ready, NT * h + n)
                        nc.scalar.activation(inter[:], keep[:, 0:VE], ACT.Copy, scale=cols[:, 1, n, h:h + 1]
                                             ).then_inc(inter_done, 1)
                    if q in now:
                        late(q)
                    for r in split_after(q):
                        hi(r)
                if kind == "mlstm" and n == NT - 1:
                    act.wait_ge(chunk_ready, NT * (h + 1))
                    act.wait_ge(sq_done, NT * h + n)
                    nc.scalar.activation(sq_junk[:], mo_sb[h % 2][:, n, :], ACT.Square,
                                         scale=rden[:, n:n + 1], accum_out=msq[:, n:n + 1]).then_inc(sq_done, 1)

        @block.vector
        def _(dve):
            steps = [0]

            def step(ins):
                ins.then_inc(v_step, 1)
                steps[0] += 1
                dve.wait_ge(v_step, steps[0])

            V = nc.vector
            TS, TT, STT = V.tensor_scalar, V.tensor_tensor, V.scalar_tensor_tensor

            def rope(q):
                z = quanta[q]
                t = (qa_sb if z.kind == "qa" else ka_sb)[z.head % 2][0:32, z.tile, :]
                d = DIL[z.tile]
                placed = lambda v: v.rearrange("p (r u) -> p r u", r=d)
                table = lambda v: v.rearrange("p (u r) -> p r u", r=d)
                step(V.stream_shuffle(tmp[32:64, :], t, list(range(16, 32)) + list(range(16))))
                step(TT(placed(t), placed(t), table(rope_sb[0:32, :]), ALU.mult))
                step(TT(placed(tmp[0:32, :]), placed(tmp[32:64, :]), table(rope_sb[32:64, :]), ALU.mult))
                TT(t, t, tmp[0:32, :], ALU.add).then_inc(rope_done, 1)
                dve.wait_ge(rope_done, rope_no[q])

            def after(q):
                z = quanta[q]
                slot = tcol(q)
                s = z.head % 2
                if z.kind == "y":
                    result(q)
                    return
                if z.kind in BY_ACT:
                    dve.wait_ge(evac, evac_no[q])
                else:
                    dve.wait_ge(pe_quantum, q + 1)
                if z.kind in ("ka", "qa"):
                    rope(q)
                elif z.kind == "za":
                    STT(za_sb[s][:], za_sb[s][:], 1.0, slot, ALU.add, ALU.mult).then_inc(post, 1)
                elif z.kind == "mz":
                    STT(mz_sb[s][:, z.tile, :], mz_sb[s][:, z.tile, :], 1.0, slot, ALU.add, ALU.mult
                        ).then_inc(post, 1)
                elif z.kind == "mv" and z.part == 1:
                    V.memset(mv_sb[s][:, :, MD:VE], 1.0).then_inc(ones_done, 1)
                elif z.kind == "mconv":
                    y = mqk[s][:, z.part, z.tile, :]
                    t = z.part * KT + z.head * 2 + z.tile
                    for d in (1, 2, 3):
                        ins = STT(y[:, d:], slot[:, 0:S - d], cw[:, t, 3 - d:4 - d], y[:, d:], ALU.mult, ALU.add)
                        if d < 3:
                            step(ins)
                    ins.then_inc(post, 1)
                    dve.wait_ge(tanh_done, conv_no[q])
                    STT(y, tmp[:], 1.0, y, ALU.add, ALU.mult).then_inc(silu_done, 1)
                elif z.kind == "pa":
                    g = ga_sb[:, z.tile, :]
                    STT(g, g, 1.0, slot, ALU.add, ALU.mult).then_inc(post, 1)
                elif z.kind == "pm":
                    g, a = gm_sb[:, z.tile, :], ga_sb[:, z.tile, :]
                    STT(g, g, 1.0, slot, ALU.add, ALU.mult).then_inc(post, 1)
                    dve.wait_ge(post, post_no[q])
                    for half in (slice(0, 512), slice(512, 1024)):
                        TT(a[:, half], a[:, half], g[:, half], ALU.add).then_inc(sum_done, 1)
                    for i, half in enumerate((slice(0, 512), slice(512, 1024))):
                        dve.wait_ge(mg_hi, 2 * z.tile + i + 1)
                        STT(mglo[:, z.tile, half], a[:, half], 0.5, mghi[:, z.tile, half].bitcast(F32),
                            ALU.mult, ALU.subtract).then_inc(mg_lo, 1)

            def lo(r):
                src, h, low = split_views(r)
                dve.wait_ge(hi_done, r + 1)
                TT(low, src, h.bitcast(F32), ALU.subtract).then_inc(vlo_done, 1)

            def result(q):
                z = quanta[q]
                if q == FIRST_Y:
                    dve.wait_ge(pw_in, 16)

                def finish(t):
                    dve.wait_ge(y_rs, t // 2 + 1)
                    STT(y_sb[:, t, :], y_sb[:, t, :], yrs[:, t:t + 1], x2_sb[:, t, :], ALU.mult, ALU.add
                        ).then_inc(y_done, 1)

                if z.tile == 3:
                    dve.wait_ge(post, post_no[q - 1])
                    dve.wait_ge(x2_in, 16)
                c = slice(z.tile * 256, (z.tile + 1) * 256)
                for i in range(2):
                    t = 4 * z.part + 2 * i
                    dve.wait_ge(sq_done, MH * NT + 4 * (q - FIRST_Y) + 2 * i + 2)
                    if z.tile == 3:
                        step(V.tensor_reduce(ysum[:, t:t + 2], ysq[:, t:t + 2, :], AX.X, ALU.add))
                        TS(ysum[:, t:t + 2], ysum[:, t:t + 2], 1.0 / DM, EPS, ALU.mult, ALU.add).then_inc(y_ms, 1)
                    TT(y_sb[:, t:t + 2, c], tcol(q)[:, 512 * i:512 * i + 512].rearrange("p (t c) -> p t c", c=256),
                       pw_sb[:, c].unsqueeze(1).broadcast_to([P, 2, 256]), ALU.mult).then_inc(post, 1)
                    if z.tile == 3:
                        dve.wait_ge(post, post_no[q] - 1 + i)
                        finish(t)
                        finish(t + 1)

            def gate_rows():
                dve.wait_ge(evac, 1)
                dve.wait_ge(const_in, 16 * NCONST)
                step(V.stream_shuffle(rows[3][:], rows[0][:], [2, 3] + list(range(2, 32))))
                step(TT(rows[0][:], rows[0][:], rows[3][:], ALU.add))
                step(V.stream_shuffle(rows[1][:], rows[0][:], [0] * 32))
                step(V.stream_shuffle(rows[2][:], rows[0][:], [1] * 32))
                step(TS(rows[1][:], rows[1][:], bg[:, 0:1], None, ALU.add))
                TS(rows[2][:], rows[2][:], bg[:, 1:2], None, ALU.add).then_inc(f_ready, 1)
                dve.wait_ge(f_ready, 1)
                step(V.memset(rows[8][:], 1.0))
                step(V.memset(rows[9][:], 0.0))
                step(V.memset(rows[8][:, 0:S:P], 0.0))
                step(V.memset(rows[9][:, 0:S:P], NEG))
                dve.wait_ge(log_done, 1)
                step(STT(rows[4][:], rows[2][:], 0.0, rows[3][:], ALU.min, ALU.subtract))
                step(V.tensor_tensor_scan(rows[5][:], rows[8][:], rows[4][:], 0.0, ALU.mult, ALU.add))
                step(TT(rows[6][:], rows[1][:], rows[5][:], ALU.subtract))
                step(V.tensor_tensor_scan(rows[7][:], rows[9][:], rows[6][:], NEG, ALU.add, ALU.max))
                bt, am, mnew, mprev, dk, bm = (srow[:, i, :] for i in (0, 1, 2, 3, 4, 6))
                step(V.tensor_copy(bt, rows[5][:, P - 1:S:P]))
                step(TT(am, bt, rows[7][:, P - 1:S:P], ALU.add))
                step(V.tensor_tensor_scan(mnew, bt, am, 0.0, ALU.add, ALU.max))
                step(V.memset(srow[:, 3, 0:1], 0.0))
                step(V.tensor_copy(srow[:, 3, 1:NT], srow[:, 2, 0:NT - 1]))
                step(TT(bm, bt, mnew, ALU.subtract))
                TT(dk, bm, mprev, ALU.add).then_inc(f_ready, 1)
                each = lambda v: v.unsqueeze(2).broadcast_to([P, NT, P])
                chunked = lambda r: r[:].rearrange("p (j l) -> p j l", l=P)
                step(TT(chunked(rows[7]), chunked(rows[7]), each(mprev), ALU.max))
                step(TS(rows[8][:], rows[7][:], -1.0, None, ALU.mult))
                step(TT(chunked(rows[0]), chunked(rows[8]), each(mprev), ALU.add))
                step(TT(chunked(rows[3]), chunked(rows[6]), each(bm), ALU.add))
                TT(rows[2][:], rows[8][:], rows[5][:], ALU.subtract).then_inc(rows_ready, 1)

            def gate_columns():
                for a in range(4):
                    for j2 in range(2):
                        i = bank_no[("cols", a, j2)]
                        dve.wait_ge(pe_bank, i + 1)
                        V.tensor_copy(cols[:, a, 4 * j2:4 * j2 + 4, :],
                                      bank[i % 3][:].rearrange("p (j h x) -> p j h x", j=4, x=32)[:, :, :, 0]
                                      ).then_inc(bank_free, 1)
                i = bank_no[("decay",)]
                dve.wait_ge(pe_bank, i + 1)
                V.tensor_copy(decay[:].rearrange("p h j -> p (h j)"), bank[i % 3][:, 0:MH * NT]
                              ).then_inc(bank_free, 1)

            def head_norm(h):
                dve.wait_ge(sq_done, NT * (h + 1))
                TS(msq[:], msq[:], 1.0 / MD, 4.0 * EPS, ALU.mult, ALU.add).then_inc(m_ms, 1)
                dve.wait_ge(m_rs, h + 1)
                step(TT(mfac[:], mrs[:], rden[:], ALU.mult))
                for j in range(NT):
                    o = mo_sb[h % 2][:, j, :]
                    ins = TS(o, o, mfac[:, j:j + 1], None, ALU.mult)
                ins.then_inc(m_norm, 1)
                dve.wait_ge(m_norm, h + 1)

            def head_gate(h):
                dve.wait_ge(post, post_no[index[("mz", h, 0, 1)]])
                for d in range(2):
                    for j2 in range(2):
                        i = bank_no[("hmT", h, d, j2)]
                        dve.wait_ge(pe_bank, i + 1)
                        z = mz_sb[h % 2][:, d, j2 * 512:(j2 + 1) * 512]
                        STT(z, bank[i % 3][:], mw[:, 2 * h + d:2 * h + d + 1], z, ALU.mult, ALU.mult
                            ).then_inc(bank_free, 1)

            def probabilities_out(h, n):
                if NT * h + n >= 2:
                    dve.wait_ge(pe_pv, NT * h + n - 1)
                for b, (first, w) in enumerate(((0, places(n)[1] + key_tiles(1, n)), (4, 1))):
                    no = bank_no[("probT", h, n, b)]
                    dve.wait_ge(pe_bank, no + 1)
                    V.tensor_copy(probT[:, n % 2, first * P:(first + w) * P], bank[no % 3][:, 0:w * P]
                                  ).then_inc(bank_free, 1)

            def compare_groups(h):
                dve.wait_ge(ml_in, 16 * NG * (h + 1))
                nm = mlc[:, :, :, 0]
                step(TT(lead[:, 0], nm[:, 0], nm[:, 1], ALU.min))
                step(TT(lead[:, 0], lead[:, 0], nm[:, 2], ALU.min))
                TT(eg[:, 0], lead[:, 0].unsqueeze(1).broadcast_to([NT, NG, P]), nm, ALU.subtract
                   ).then_inc(lead_done, 1)

            def group_shares(h):
                dve.wait_ge(eg_done, h + 1)
                step(TT(eg[:, 1], eg[:, 0], mlc[:, :, :, 1], ALU.mult))
                step(TT(lead[:, 1], eg[:, 1, 0], eg[:, 1, 1], ALU.add))
                step(TT(lead[:, 1], lead[:, 1], eg[:, 1, 2], ALU.add))
                step(V.reciprocal(lead[:, 1], lead[:, 1]))
                TT(eg[:, 2], eg[:, 0], lead[:, 1].unsqueeze(1).broadcast_to([NT, NG, P]), ALU.mult
                   ).then_inc(share_done, 1)

            def combine_groups(h):
                dve.wait_ge(share_in, 16 * (h + 1))
                dve.wait_ge(out_done, NT * (h + 1))
                dve.wait_ge(post, post_no[index[("za", h, 0, 0)]])
                o, z = qa_sb[h % 2], za_sb[h % 2][:]
                by_token = lambda v, d: v.rearrange("p (r u) -> p u r", r=d)
                for g, d in enumerate(DIL):
                    share = share_sb[:, g, :].rearrange("p (u r) -> p u r", r=d)
                    step(TT(share, share, by_token(o[:, g, :], d), ALU.mult))
                step(TT(share_sb[:, 0, :], share_sb[:, 0, :], share_sb[:, 1, :], ALU.add))
                step(TT(share_sb[:, 0, :], share_sb[:, 0, :], share_sb[:, 2, :], ALU.add))
                STT(z, share_sb[:, 0, :], 0.5, z, ALU.mult, ALU.mult).then_inc(att_done, 1)

            dve.wait_ge(start_in, 16 * NSTART)
            dve.wait_ge(g_ready, 2)
            step(V.tensor_copy(raw[:, 0, :, 0:P:32], ifw[:, :, 0:MH]))
            V.tensor_copy(raw[:, 0, :, 1:P:32], ifw[:, :, MH:2 * MH]).then_inc(if_ready, 1)
            def hidden_lo(i):
                kt, n2 = ht_order[i]
                dve.wait_ge(ht_hi, i + 1)
                part = slice(n2 * 512, (n2 + 1) * 512)
                STT(hlo[:, kt, part], ht_bank[kt], prew[:, kt:kt + 1], hhi[:, kt, part].bitcast(F32),
                    ALU.mult, ALU.subtract).then_inc(bank_free, 1)

            def gate_weights_lo():
                dve.wait_ge(hi_done, 1)
                for c in range(2):
                    ins = TT(whi[:, wslot(0), :, 2 + c:P:32], raw[:, 0, :, c:P:32],
                             whi[:, wslot(0), :, c:P:32].bitcast(F32), ALU.subtract)
                ins.then_inc(vlo_done, 1)

            def mean_square(t):
                dve.wait_ge(x_sq, t + 1)
                TS(ssq[:, t:t + 1], ssq[:, t:t + 1], 1.0 / DM, EPS, ALU.mult, ALU.add).then_inc(x_ms, 1)

            mean_square(0)
            for t in range(NT):
                if t + 1 < NT:
                    mean_square(t + 1)
                if t == 5:
                    gate_weights_lo()
                dve.wait_ge(x_rs, t + 1)
                TS(x_sb[:, t, :], x_sb[:, t, :], ssq[:, NT + t:NT + t + 1], None, ALU.mult).then_inc(x_norm, 1)
            for i in range(2 * KT):
                hidden_lo(i)
            dve.wait_ge(const_in, 16 * NCONST)
            for part, f in ((0, 0.5), (1, 1.0 / 32.0)):
                tiles = slice(part * KT, (part + 1) * KT)
                step(TS(cw[:, tiles, :], cw[:, tiles, :], f, None, ALU.mult))
                step(TS(cb[:, tiles], cb[:, tiles], f, None, ALU.mult))
            TS(mw[:], mw[:], 0.5, None, ALU.mult).then_inc(cw_ready, 1)
            last_qs = []
            waiting = []
            for kind, h, n, qs in slots:
                if kind == "start":
                    gate_rows()
                    continue
                if (kind == "mlstm" and h and n == 1) or (kind == "tail" and n == 1):
                    head_gate(h - 1 if kind == "mlstm" else MH - 1)
                for back, ht, nt in att_tiles(kind, h, n):
                    if back == 1:
                        probabilities_out(ht, nt)
                if kind == "att":
                    if h >= 2 and n == 0:
                        dve.wait_ge(ml_out, 16 * (h - 1))
                    for g in range(NG):
                        no = bank_no[("score", h, n, g // 2)]
                        dve.wait_ge(pe_bank, no + 1)
                        m, place = key_tiles(g, n), places(n)[g]
                        mask = mask_sb[:, 2 * P:3 * P] if g == 2 else mask_sb[:, (2 - m) * P:2 * P]
                        ins = V.tensor_tensor_reduce(
                            out=prob[:, n % 2, place * P:(place + m) * P],
                            in0=bank[no % 3][:, place % 4 * P:(place % 4 + m) * P], in1=mask,
                            scale=1.0, scalar=-3.0e38, op0=ALU.add, op1=ALU.max, accum_out=pmax[:, g:g + 1])
                        if g:
                            ins.then_inc(bank_free, 1)
                    dve.wait_ge(bank_free, no + 1)
                    TS(ml[:, h % 2, :, n, 0], pmax[:, 0:NG], -ASCALE, None, ALU.mult).then_inc(max_done, 1)
                hp = h - 1 if kind == "att" else AH - 1
                if kind == "fill" and n == 3:
                    gate_columns()
                if hp >= 0 and (kind == "att" or (kind == "mlstm" and h == 0)):
                    if n == 1:
                        compare_groups(hp)
                    if n == 2:
                        group_shares(hp)
                    if n == 4:
                        combine_groups(hp)
                if kind == "mlstm":
                    c = NT * h + n
                    no = bank_no[("qk", h, n)]
                    if n == 0:
                        dve.wait_ge(g_in, 16 * (h + 1))
                    if c:
                        dve.wait_ge(e_done, c)
                    TT(dmat[:], neg_g[h % 2][:, n * P:(n + 1) * P], tril[:], ALU.add).then_inc(d_done, 1)
                    dve.wait_ge(pe_bank, no + 1)
                    dve.wait_ge(e_done, c + 1)
                    TT(wmat[:], bank[no % 3][:, 0:P], emat[:], ALU.mult).then_inc(bank_free, 1)
                for q in waiting:
                    after(q)
                if (kind == "mlstm" and h and n == 0) or (kind == "tail" and n == 0):
                    head_norm(h - 1 if kind == "mlstm" else MH - 1)
                now, waiting = (qs, []) if kind in ("fill", "tail") else (qs[:-1], qs[-1:])
                for q in now:
                    after(q)
                    if kind == "tail":
                        for r in split_after(q):
                            if loads[r][0] != "w":
                                lo(r)
                for q in last_qs:
                    z = quanta[q]
                    if z.kind == "va":
                        for j2 in range(2):
                            no = bank_no[("vT", q, j2)]
                            dve.wait_ge(pe_bank, no + 1)
                            V.tensor_copy(va_sb[z.head % 2][:, z.tile, j2 * 512:(j2 + 1) * 512], bank[no % 3][:]
                                          ).then_inc(bank_free, 1)
                last_qs = qs
                if kind == "mlstm":
                    no = bank_no[("B", h, n)]
                    dve.wait_ge(pe_bank, no + 1)
                    if n:
                        dve.wait_ge(inter_done, (NT - 1) * h + n)
                        TT(total[:], inter[:], bank[no % 3][:, 0:VE], ALU.add).then_inc(bank_free, 1)
                    else:
                        V.tensor_copy(total[:], bank[no % 3][:, 0:VE]).then_inc(bank_free, 1)
                    dve.wait_ge(bank_free, no + 1)
                    dl = total[:, MD:VE]
                    step(STT(den[:, 0:1], dl, -1.0, dl, ALU.mult, ALU.max))
                    step(TT(den[:, 1:2], den[:, 0:1], cols[:, 3, n, h:h + 1], ALU.max))
                    step(V.reciprocal(rden[:, n:n + 1], den[:, 1:2]))
                    if n == 0:
                        dve.wait_ge(evac, evac_no[index[("mo", h, 1, 0)]])
                    o = mo_sb[h % 2][:, n, :]
                    STT(o, o, 1.0, total[:, 0:MD], ALU.add, ALU.mult).then_inc(chunk_ready, 1)
                    dve.wait_ge(chunk_ready, NT * h + n + 1)
                    if n < NT - 1:
                        for d in range(2):
                            no = bank_no[("C", h, n, d)]
                            dve.wait_ge(pe_bank, no + 1)
                            if n:
                                STT(state[:, d, :], state[:, d, :], decay[:, h, n:n + 1], bank[no % 3][:, 0:VE],
                                    ALU.mult, ALU.add).then_inc(bank_free, 1)
                            else:
                                V.tensor_copy(state[:, d, :], bank[no % 3][:, 0:VE]).then_inc(bank_free, 1)


def constants():
    i = np.arange(P)
    query, key = i[:, None], i[None, :]
    residue = S // DIL[2]
    seen = np.concatenate([key >= query, key <= query,
                           (key <= query) & (key // residue == query // residue)], axis=1)
    mask = np.where(seen, 0.0, NEG).astype(np.float32)
    tril = np.where(i[:, None] <= i[None, :], 0.0, NEG).astype(np.float32)
    half = AD // 8
    freq = np.float32(500000.0) ** (-np.arange(0, 2 * half, 2, dtype=np.float32) / np.float32(2 * half))
    ang = (np.arange(S, dtype=np.float32)[:, None] * freq[None, :].astype(np.float32)).astype(np.float32)
    cos, sin = np.cos(ang).T, np.sin(ang).T
    rope = np.concatenate([cos, cos, -sin, sin]).astype(np.float32)
    return np.eye(P, dtype=np.float32), (mask.view(np.uint32) >> 16).astype(np.uint16), tril, rope


def kernel(x, pre_norm_w, w_in, b_if, conv_w, conv_b, m_norm_w, w_proj_m, w_proj_a, w_out, post_norm_w):
    import concourse.bacc as bacc
    from concourse.bass_utils import run_bass_kernel_spmd

    a = np.ascontiguousarray
    by_tile = lambda v: a(np.asarray(v).reshape(-1, P).T)
    eye, mask, tril, rope = constants()
    b = np.asarray(b_if)[0]
    arrays = {
        "x_in": a(np.asarray(x)[0]),
        "w_in": a(np.asarray(w_in)[0]),
        "w_pm": a(np.asarray(w_proj_m)[0]),
        "w_pa": a(np.asarray(w_proj_a)[0]),
        "w_out": a(np.asarray(w_out)[0]),
        "b_gate": a(np.stack([np.repeat(b[:MH], 32), np.repeat(b[MH:], 32)], 1)),
        "conv_wt": a(np.asarray(conv_w)[0].reshape(4, 16, P).transpose(2, 1, 0)),
        "conv_bt": by_tile(np.asarray(conv_b)[0]),
        "pre_wt": by_tile(np.asarray(pre_norm_w)[0]),
        "m_wt": by_tile(np.asarray(m_norm_w)[0]),
        "post_w": a(np.asarray(post_norm_w)[0]),
        "c_ident": eye, "c_mask": mask, "c_tril": tril, "c_rope": rope,
    }
    nc = bacc.Bacc("TRN2", target_bir_lowering=False, num_devices=1, dynamic_dma_scratch_size=1024)
    args = [nc.dram_tensor(n, v.shape, mybir.dt.from_np(v.dtype), kind="ExternalInput").ap()
            for n, v in arrays.items()]
    args.append(nc.dram_tensor("out", (S, DM), F32, kind="ExternalOutput").ap())
    hybrid_kernel(nc, *args)
    r = run_bass_kernel_spmd(nc, [arrays], core_ids=[0])
    return r.results[0]["out"].reshape(1, S, DM)
```
